# Optimizing a Trainium2 kernel written in Bass

```python
import jax, jax.numpy as jnp
from jax import lax
import numpy as np
import math

D_MODEL = 1024
BATCH = 1
SEQ = 256
DEPTH = 2

HEAD_DIM = 64
MIX_WIDTH = D_MODEL
MOBA_HEADS = 6
MLSTM_HEADS = 4
SWA_Q_HEADS = 6
SWA_KV_HEADS = 2
MOBA_WIDTH = MOBA_HEADS * HEAD_DIM
MLSTM_WIDTH = MLSTM_HEADS * HEAD_DIM
SWA_Q_WIDTH = SWA_Q_HEADS * HEAD_DIM
SWA_KV_WIDTH = SWA_KV_HEADS * HEAD_DIM
MOBA_BLOCK = 256
MOBA_TOPK = 3
MOBA_Q_CHUNK = 64
MLSTM_CHUNK = 64
CONV_WIDTH = 4
SWA_WINDOW = 128
ROPE_THETA = 10000.0
D_FF = 4 * D_MODEL
NORM_EPS = 1e-6
IN_SPLITS = (MOBA_WIDTH, MOBA_WIDTH, MOBA_WIDTH, SWA_Q_WIDTH, SWA_KV_WIDTH, SWA_KV_WIDTH, 2 * MLSTM_WIDTH, MLSTM_WIDTH, MLSTM_WIDTH, MLSTM_HEADS, MLSTM_HEADS)
IN_WIDTH = sum(IN_SPLITS)


def rms_norm(x, g):
    xf = x.astype(jnp.float32)
    y = xf * lax.rsqrt(jnp.mean(xf * xf, axis=-1, keepdims=True) + NORM_EPS)
    return (y * g.astype(jnp.float32)).astype(x.dtype)

def rope_tables(seq):
    inv = ROPE_THETA ** (-jnp.arange(0, HEAD_DIM, 2, dtype=jnp.float32) / HEAD_DIM)
    ang = jnp.arange(seq, dtype=jnp.float32)[:, None] * inv[None, :]
    return jnp.cos(ang), jnp.sin(ang)

def apply_rope(x, cos, sin):
    c = cos[:, None, :].astype(x.dtype)
    s = sin[:, None, :].astype(x.dtype)
    x1, x2 = jnp.split(x, 2, axis=-1)
    return jnp.concatenate([x1 * c - x2 * s, x2 * c + x1 * s], axis=-1)

def causal_depthwise_conv(x, w, b):
    C = x.shape[-1]
    y = lax.conv_general_dilated(x, w[:, None, :].astype(x.dtype), (1,), [(w.shape[0] - 1, 0)],
                                 dimension_numbers=('NWC', 'WIO', 'NWC'), feature_group_count=C)
    return y + b.astype(x.dtype)

def moba_attention(q, k, v):
    B, H, S, D = q.shape
    L = MOBA_BLOCK
    n_blocks = -(-S // L)
    s_pad = n_blocks * L
    if s_pad != S:
        padw = ((0, 0), (0, 0), (0, s_pad - S), (0, 0))
        q, k, v = jnp.pad(q, padw), jnp.pad(k, padw), jnp.pad(v, padw)
    k_blk = k.reshape(B, H, n_blocks, L, D)
    v_blk = v.reshape(B, H, n_blocks, L, D)
    k_mean = jnp.mean(k_blk.astype(jnp.float32), axis=3)
    top = min(MOBA_TOPK, n_blocks)
    scale = D ** -0.5
    Qc = MOBA_Q_CHUNK
    b_idx = jnp.arange(B)[:, None, None, None]
    h_idx = jnp.arange(H)[None, :, None, None]

    def one_chunk(c):
        start = c * Qc
        blk = start // L
        qc = lax.dynamic_slice_in_dim(q, start, Qc, axis=2)
        gate = jnp.einsum('bhqd,bhnd->bhqn', qc.astype(jnp.float32), k_mean)
        gate = jnp.where(jnp.arange(n_blocks) < blk, gate, -jnp.inf)
        _, sel = lax.top_k(gate, top)
        sel_ok = jnp.arange(top) < blk
        k_sel = k_blk[b_idx, h_idx, sel]
        v_sel = v_blk[b_idx, h_idx, sel]
        s_sel = jnp.einsum('bhqd,bhqrld->bhqrl', qc, k_sel).astype(jnp.float32) * scale
        s_sel = jnp.where(sel_ok[:, None], s_sel, -jnp.inf).reshape(B, H, Qc, top * L)
        k_own = lax.dynamic_slice_in_dim(k, blk * L, L, axis=2)
        v_own = lax.dynamic_slice_in_dim(v, blk * L, L, axis=2)
        s_own = jnp.einsum('bhqd,bhld->bhql', qc, k_own).astype(jnp.float32) * scale
        q_pos = start + jnp.arange(Qc)
        k_pos = blk * L + jnp.arange(L)
        s_own = jnp.where(k_pos[None, :] <= q_pos[:, None], s_own, -jnp.inf)
        p = jax.nn.softmax(jnp.concatenate([s_sel, s_own], axis=-1), axis=-1).astype(v.dtype)
        p_sel = p[..., :top * L].reshape(B, H, Qc, top, L)
        p_own = p[..., top * L:]
        return (jnp.einsum('bhqrl,bhqrld->bhqd', p_sel, v_sel)
                + jnp.einsum('bhql,bhld->bhqd', p_own, v_own))

    outs = lax.map(one_chunk, jnp.arange(s_pad // Qc))
    out = jnp.moveaxis(outs, 0, 2).reshape(B, H, s_pad, D)
    return out[:, :, :S]

def mlstm_chunkwise(q, k, v, i_pre, f_pre):
    B, H, S, D = q.shape
    L = MLSTM_CHUNK
    nc = S // L
    k = k * (D ** -0.5)
    log_f = jax.nn.log_sigmoid(f_pre)

    def chunks(a):
        return jnp.moveaxis(a.reshape(B, H, nc, L, *a.shape[3:]), 2, 0)

    causal = jnp.tril(jnp.ones((L, L), dtype=bool))

    def step(carry, inp):
        C, n, m = carry
        qc, kc, vc, ic, lfc = inp
        b = jnp.cumsum(lfc, axis=-1)
        a = b[..., -1]
        d = b[..., :, None] - b[..., None, :] + ic[..., None, :]
        d = jnp.where(causal, d, -jnp.inf)
        inter = b + m[..., None]
        m_t = jnp.maximum(inter, jnp.max(d, axis=-1))
        w_intra = jnp.exp(d - m_t[..., None])
        w_inter = jnp.exp(inter - m_t)
        qk = jnp.einsum('bhtd,bhsd->bhts', qc, kc) * w_intra
        num = (w_inter[..., None] * jnp.einsum('bhtd,bhde->bhte', qc, C)
               + jnp.einsum('bhts,bhse->bhte', qk, vc))
        den = w_inter * jnp.einsum('bhtd,bhd->bht', qc, n) + jnp.sum(qk, axis=-1)
        h = num / jnp.maximum(jnp.abs(den), jnp.exp(-m_t))[..., None]
        g = a[..., None] - b + ic
        m_new = jnp.maximum(a + m, jnp.max(g, axis=-1))
        w_s = jnp.exp(g - m_new[..., None])
        decay = jnp.exp(a + m - m_new)
        C_new = decay[..., None, None] * C + jnp.einsum('bhsd,bhse->bhde', kc * w_s[..., None], vc)
        n_new = decay[..., None] * n + jnp.einsum('bhs,bhsd->bhd', w_s, kc)
        return (C_new, n_new, m_new), h

    init = (jnp.zeros((B, H, D, D), jnp.float32), jnp.zeros((B, H, D), jnp.float32),
            jnp.zeros((B, H), jnp.float32))
    _, h = lax.scan(step, init, (chunks(q), chunks(k), chunks(v), chunks(i_pre), chunks(log_f)))
    return jnp.moveaxis(h, 0, 2).reshape(B, H, S, D)

def swa_attention(q, k, v, sinks):
    B, S, Hq, D = q.shape
    Hkv = k.shape[2]
    G = Hq // Hkv
    W = SWA_WINDOW
    nb = S // W
    qb = q.reshape(B, nb, W, Hkv, G, D)

    def band(a):
        ab = a.reshape(B, nb, W, Hkv, D)
        prev = jnp.pad(ab, ((0, 0), (1, 0), (0, 0), (0, 0), (0, 0)))[:, :-1]
        return jnp.concatenate([prev, ab], axis=2)

    kb, vb = band(k), band(v)
    s = jnp.einsum('bnqkgd,bnjkd->bnkgqj', qb, kb).astype(jnp.float32) * (D ** -0.5)
    qi = jnp.arange(W)[:, None] + W
    kj = jnp.arange(2 * W)[None, :]
    in_window = (qi - kj >= 0) & (qi - kj < W)
    exists = (jnp.arange(nb)[:, None, None] > 0) | (kj[None] >= W)
    mask = in_window[None] & exists
    s = jnp.where(mask[None, :, None, None], s, -jnp.inf)
    sink = jnp.broadcast_to(sinks.astype(jnp.float32).reshape(1, 1, Hkv, G, 1, 1), s.shape[:-1] + (1,))
    p = jax.nn.softmax(jnp.concatenate([s, sink], axis=-1), axis=-1)[..., :-1].astype(v.dtype)
    o = jnp.einsum('bnkgqj,bnjkd->bnqkgd', p, vb)
    return o.reshape(B, S, Hq, D)

def hybrid_layer(x, cos, sin, ln1, w_in, conv_w, conv_b, igate_b, fgate_b, mlstm_norm,
                 moba_q_norm, moba_k_norm, swa_q_norm, swa_k_norm, swa_sinks, w_out,
                 ln2, w_up, w_down):
    B, S, _ = x.shape
    hn = rms_norm(x, ln1)
    proj = hn @ w_in
    idx = np.cumsum(IN_SPLITS)[:-1].tolist()
    mq, mk, mv, sq, sk, sv, xqk, xv, xo, xi, xf = jnp.split(proj, idx, axis=-1)

    def heads(a):
        return a.reshape(B, S, -1, HEAD_DIM)

    def bhsd(a):
        return a.transpose(0, 2, 1, 3)

    mq = apply_rope(rms_norm(heads(mq), moba_q_norm), cos, sin)
    mk = apply_rope(rms_norm(heads(mk), moba_k_norm), cos, sin)
    y_moba = bhsd(moba_attention(bhsd(mq), bhsd(mk), bhsd(heads(mv)))).reshape(B, S, MOBA_WIDTH)

    qk = jax.nn.silu(causal_depthwise_conv(xqk, conv_w, conv_b))
    lq, lk = jnp.split(qk, 2, axis=-1)
    i_pre = (xi + igate_b).astype(jnp.float32).transpose(0, 2, 1)
    f_pre = (xf + fgate_b).astype(jnp.float32).transpose(0, 2, 1)
    h = mlstm_chunkwise(bhsd(heads(lq)).astype(jnp.float32), bhsd(heads(lk)).astype(jnp.float32),
                        bhsd(heads(xv)).astype(jnp.float32), i_pre, f_pre)
    h = bhsd(h).astype(x.dtype) * heads(jax.nn.sigmoid(xo))
    y_mlstm = rms_norm(h, mlstm_norm).reshape(B, S, MLSTM_WIDTH)

    sq = apply_rope(rms_norm(heads(sq), swa_q_norm), cos, sin)
    sk = apply_rope(rms_norm(heads(sk), swa_k_norm), cos, sin)
    y_swa = swa_attention(sq, sk, heads(sv), swa_sinks).reshape(B, S, SWA_Q_WIDTH)

    x = x + jnp.concatenate([y_moba, y_mlstm, y_swa], axis=-1) @ w_out
    u = rms_norm(x, ln2) @ w_up
    return x + jnp.square(jax.nn.relu(u)) @ w_down

def first_inputs(seed: int = 0) -> dict:
    key = jax.random.key(seed)
    ks = jax.random.split(key, 17)
    f32 = jnp.float32

    def nrm(k, shape, scale):
        return jax.random.normal(k, shape, f32) * scale

    return {
        'x': nrm(ks[0], (BATCH, SEQ, D_MODEL), 1.0),
        'ln1': 1.0 + nrm(ks[1], (DEPTH, D_MODEL), 0.02),
        'w_in': nrm(ks[2], (DEPTH, D_MODEL, IN_WIDTH), D_MODEL ** -0.5),
        'conv_w': nrm(ks[3], (DEPTH, CONV_WIDTH, 2 * MLSTM_WIDTH), CONV_WIDTH ** -0.5),
        'conv_b': nrm(ks[4], (DEPTH, 2 * MLSTM_WIDTH), 0.02),
        'igate_b': nrm(ks[5], (DEPTH, MLSTM_HEADS), 0.1),
        'fgate_b': jnp.linspace(3.0, 6.0, MLSTM_HEADS, dtype=f32)[None] + nrm(ks[6], (DEPTH, MLSTM_HEADS), 0.1),
        'mlstm_norm': 1.0 + nrm(ks[7], (DEPTH, MLSTM_HEADS, HEAD_DIM), 0.02),
        'moba_q_norm': 1.0 + nrm(ks[8], (DEPTH, HEAD_DIM), 0.02),
        'moba_k_norm': 1.0 + nrm(ks[9], (DEPTH, HEAD_DIM), 0.02),
        'swa_q_norm': 1.0 + nrm(ks[10], (DEPTH, HEAD_DIM), 0.02),
        'swa_k_norm': 1.0 + nrm(ks[11], (DEPTH, HEAD_DIM), 0.02),
        'swa_sinks': nrm(ks[12], (DEPTH, SWA_Q_HEADS), 1.0),
        'w_out': nrm(ks[13], (DEPTH, MIX_WIDTH, D_MODEL), MIX_WIDTH ** -0.5),
        'ln2': 1.0 + nrm(ks[14], (DEPTH, D_MODEL), 0.02),
        'w_up': nrm(ks[15], (DEPTH, D_MODEL, D_FF), D_MODEL ** -0.5),
        'w_down': nrm(ks[16], (DEPTH, D_FF, D_MODEL), D_FF ** -0.5),
    }

def first_block(x, ln1, w_in, conv_w, conv_b, igate_b, fgate_b, mlstm_norm, moba_q_norm,
              moba_k_norm, swa_q_norm, swa_k_norm, swa_sinks, w_out, ln2, w_up, w_down):
    cos, sin = rope_tables(x.shape[1])
    for l in range(DEPTH):
        x = hybrid_layer(x, cos, sin, ln1[l], w_in[l], conv_w[l], conv_b[l], igate_b[l], fgate_b[l],
                         mlstm_norm[l], moba_q_norm[l], moba_k_norm[l], swa_q_norm[l], swa_k_norm[l],
                         swa_sinks[l], w_out[l], ln2[l], w_up[l], w_down[l])
    return x


GRID_W = 64
NA_HEADS = 8
NA_HEAD_DIM = 64
NA_WIN_ROWS = 8
NA_WIN_COLS = 16
NA_QCOL_BLOCK = NA_WIN_COLS
NA_KCOL_BLOCK = 2 * NA_WIN_COLS
SW_HEADS = 8
SW_KV_HEADS = 2
SW_HEAD_DIM = 64
SW_WINDOW = 128
SW_BLOCK = 128
REL_BUCKETS = 32
REL_MAX_DIST = 128
D_FF_2 = 2816
N_BRANCHES = 2
EPS = 1e-6
NEG = -1e30

NA_WIDTH = NA_HEADS * NA_HEAD_DIM
SW_Q_WIDTH = SW_HEADS * SW_HEAD_DIM
SW_KV_WIDTH = SW_KV_HEADS * SW_HEAD_DIM
IN_WIDTH_2 = 3 * NA_WIDTH + SW_Q_WIDTH + 2 * SW_KV_WIDTH + N_BRANCHES * D_MODEL


def rms_norm_2(x, g):
    xf = x.astype(jnp.float32)
    y = xf * lax.rsqrt(jnp.mean(xf * xf, axis=-1, keepdims=True) + EPS)
    return (y * g.astype(jnp.float32)).astype(x.dtype)

def swiglu(x, w_gate, w_up, w_down):
    return (jax.nn.silu(x @ w_gate) * (x @ w_up)) @ w_down

def t5_bucket(rel):
    nb = REL_BUCKETS // 2
    max_exact = nb // 2
    n = np.abs(rel)
    large = max_exact + (np.log(np.maximum(n, 1) / max_exact)
                         / np.log(REL_MAX_DIST / max_exact) * (nb - max_exact)).astype(np.int32)
    large = np.minimum(large, nb - 1)
    return ((rel > 0) * nb + np.where(n < max_exact, n, large)).astype(np.int32)

def neighbourhood_attention(q, k, v, rpb):
    B, S, H, dh = q.shape
    rows = S // GRID_W
    kr = min(NA_WIN_ROWS, rows)
    ncb = GRID_W // NA_QCOL_BLOCK
    r = np.arange(rows)
    row_start = np.clip(r - kr // 2, 0, rows - kr)
    key_rows = row_start[:, None] + np.arange(kr)
    cb = np.arange(ncb)
    kcol_start = np.clip(cb * NA_QCOL_BLOCK - NA_WIN_COLS // 2, 0, GRID_W - NA_KCOL_BLOCK)
    key_cols = kcol_start[:, None] + np.arange(NA_KCOL_BLOCK)
    key_idx = (key_rows[:, None, :, None] * GRID_W + key_cols[None, :, None, :])
    key_idx = key_idx.reshape(rows, ncb, kr * NA_KCOL_BLOCK)
    kg = k[:, key_idx]
    vg = v[:, key_idx]
    qb = q.reshape(B, rows, ncb, NA_QCOL_BLOCK, H, dh)
    s = jnp.einsum('brcqhd,brckhd->bhrcqk', qb, kg).astype(jnp.float32) / math.sqrt(dh)
    q_cols = cb[:, None] * NA_QCOL_BLOCK + np.arange(NA_QCOL_BLOCK)
    q_col_start = np.clip(q_cols - NA_WIN_COLS // 2, 0, GRID_W - NA_WIN_COLS)
    kc = key_cols[:, None, :]
    col_ok = (kc >= q_col_start[..., None]) & (kc < q_col_start[..., None] + NA_WIN_COLS)
    row_idx = key_rows - r[:, None] + NA_WIN_ROWS - 1
    col_idx = np.clip(kc - q_cols[..., None] + NA_WIN_COLS - 1, 0, 2 * NA_WIN_COLS - 2)
    bias = rpb[:, row_idx[:, None, None, :, None], col_idx[None, :, :, None, :]]
    bias = bias.reshape(H, rows, ncb, NA_QCOL_BLOCK, kr * NA_KCOL_BLOCK)
    mask = np.broadcast_to(col_ok[None, :, :, None, :],
                           (rows, ncb, NA_QCOL_BLOCK, kr, NA_KCOL_BLOCK))
    mask = mask.reshape(rows, ncb, NA_QCOL_BLOCK, kr * NA_KCOL_BLOCK)
    s = jnp.where(mask, s + bias.astype(jnp.float32), NEG)
    p = jax.nn.softmax(s, axis=-1)
    o = jnp.einsum('bhrcqk,brckhd->brcqhd', p.astype(v.dtype), vg)
    return o.reshape(B, S, H * dh)

def sliding_window_gqa(q, k, v, rel_bias, sink):
    B, S, _, dh = q.shape
    nb = S // SW_BLOCK
    rep = SW_HEADS // SW_KV_HEADS
    qb = q.reshape(B, nb, SW_BLOCK, SW_KV_HEADS, rep, dh)
    pad = ((0, 0), (SW_BLOCK, SW_BLOCK), (0, 0), (0, 0))
    kp = jnp.pad(k, pad).reshape(B, nb + 2, SW_BLOCK, SW_KV_HEADS, dh)
    vp = jnp.pad(v, pad).reshape(B, nb + 2, SW_BLOCK, SW_KV_HEADS, dh)
    kb = jnp.concatenate([kp[:, :-2], kp[:, 1:-1], kp[:, 2:]], axis=2)
    vb = jnp.concatenate([vp[:, :-2], vp[:, 1:-1], vp[:, 2:]], axis=2)
    s = jnp.einsum('bnqgrd,bnkgd->bgrnqk', qb, kb).astype(jnp.float32) / math.sqrt(dh)
    a = np.arange(SW_BLOCK)[:, None]
    j = np.arange(3 * SW_BLOCK)[None, :]
    rel = j - SW_BLOCK - a
    kpos = (np.arange(nb)[:, None, None] - 1) * SW_BLOCK + j[None]
    mask = (np.abs(rel)[None] <= SW_WINDOW) & (kpos >= 0) & (kpos < S)
    bias = rel_bias.astype(jnp.float32).reshape(SW_KV_HEADS, rep, 1, SW_BLOCK, 3 * SW_BLOCK)
    s = jnp.where(mask, s + bias, NEG)
    sink_b = sink.astype(jnp.float32).reshape(SW_KV_HEADS, rep, 1, 1, 1)
    m = jnp.maximum(s.max(axis=-1, keepdims=True), sink_b)
    e = jnp.exp(s - m)
    p = e / (e.sum(axis=-1, keepdims=True) + jnp.exp(sink_b - m))
    o = jnp.einsum('bgrnqk,bnkgd->bnqgrd', p.astype(v.dtype), vb)
    return o.reshape(B, S, SW_HEADS * dh)

def second_inputs(seed: int = 0) -> dict:
    key = jax.random.key(seed)
    ks = jax.random.split(key, 24)
    L, D, F = DEPTH, D_MODEL, D_FF_2
    nrm = lambda k, shape, fan: jax.random.normal(k, shape, jnp.float32) * fan ** -0.5
    gain = lambda k, shape: 1.0 + 0.05 * jax.random.normal(k, shape, jnp.float32)
    return {
        "x": jax.random.normal(ks[0], (BATCH, SEQ, D), jnp.float32),
        "ffn1_norm": gain(ks[1], (L, D)),
        "ffn1_w_gate": nrm(ks[2], (L, D, F), D),
        "ffn1_w_up": nrm(ks[3], (L, D, F), D),
        "ffn1_w_down": nrm(ks[4], (L, F, D), F),
        "mix_norm": gain(ks[5], (L, D)),
        "w_in": nrm(ks[6], (L, D, IN_WIDTH_2), D),
        "b_gate": 0.01 * jax.random.normal(ks[7], (L, N_BRANCHES * D), jnp.float32),
        "na_q_norm": gain(ks[8], (L, NA_HEAD_DIM)),
        "na_k_norm": gain(ks[9], (L, NA_HEAD_DIM)),
        "na_rpb": 0.1 * jax.random.normal(ks[10], (L, NA_HEADS, 2 * NA_WIN_ROWS - 1, 2 * NA_WIN_COLS - 1), jnp.float32),
        "sw_q_norm": gain(ks[11], (L, SW_HEAD_DIM)),
        "sw_k_norm": gain(ks[12], (L, SW_HEAD_DIM)),
        "sw_sink": 0.5 * jax.random.normal(ks[13], (L, SW_HEADS), jnp.float32),
        "t5_rel_table": 0.1 * jax.random.normal(ks[14], (REL_BUCKETS, SW_HEADS), jnp.float32),
        "w_branch_na": nrm(ks[15], (L, NA_WIDTH, D), NA_WIDTH),
        "w_branch_sw": nrm(ks[16], (L, SW_Q_WIDTH, D), SW_Q_WIDTH),
        "w_out": nrm(ks[17], (L, D, D), D),
        "ffn2_norm": gain(ks[18], (L, D)),
        "ffn2_w_gate": nrm(ks[19], (L, D, F), D),
        "ffn2_w_up": nrm(ks[20], (L, D, F), D),
        "ffn2_w_down": nrm(ks[21], (L, F, D), F),
    }

def second_block(x, ffn1_norm, ffn1_w_gate, ffn1_w_up, ffn1_w_down, mix_norm, w_in, b_gate,
              na_q_norm, na_k_norm, na_rpb, sw_q_norm, sw_k_norm, sw_sink, t5_rel_table,
              w_branch_na, w_branch_sw, w_out, ffn2_norm, ffn2_w_gate, ffn2_w_up, ffn2_w_down):
    B, S, D = x.shape
    rel = np.arange(3 * SW_BLOCK)[None, :] - SW_BLOCK - np.arange(SW_BLOCK)[:, None]
    t5_bias = jnp.transpose(t5_rel_table[t5_bucket(rel)], (2, 0, 1))
    splits = np.cumsum([NA_WIDTH, NA_WIDTH, NA_WIDTH, SW_Q_WIDTH, SW_KV_WIDTH, SW_KV_WIDTH])
    for l in range(DEPTH):
        x = x + 0.5 * swiglu(rms_norm_2(x, ffn1_norm[l]), ffn1_w_gate[l], ffn1_w_up[l], ffn1_w_down[l])
        h = rms_norm_2(x, mix_norm[l])
        z = h @ w_in[l]
        qa, ka, va, qs, ks_, vs, zg = jnp.split(z, splits, axis=-1)
        qa = rms_norm_2(qa.reshape(B, S, NA_HEADS, NA_HEAD_DIM), na_q_norm[l])
        ka = rms_norm_2(ka.reshape(B, S, NA_HEADS, NA_HEAD_DIM), na_k_norm[l])
        va = va.reshape(B, S, NA_HEADS, NA_HEAD_DIM)
        o_na = neighbourhood_attention(qa, ka, va, na_rpb[l])
        qs = rms_norm_2(qs.reshape(B, S, SW_HEADS, SW_HEAD_DIM), sw_q_norm[l])
        ks_ = rms_norm_2(ks_.reshape(B, S, SW_KV_HEADS, SW_HEAD_DIM), sw_k_norm[l])
        vs = vs.reshape(B, S, SW_KV_HEADS, SW_HEAD_DIM)
        o_sw = sliding_window_gqa(qs, ks_, vs, t5_bias, sw_sink[l])
        g = jax.nn.sigmoid((zg + b_gate[l]).astype(jnp.float32)).astype(x.dtype)
        g = g.reshape(B, S, N_BRANCHES, D)
        merged = g[:, :, 0] * (o_na @ w_branch_na[l]) + g[:, :, 1] * (o_sw @ w_branch_sw[l])
        x = x + merged @ w_out[l]
        x = x + 0.5 * swiglu(rms_norm_2(x, ffn2_norm[l]), ffn2_w_gate[l], ffn2_w_up[l], ffn2_w_down[l])
    return x


def setup_inputs(seed=0):
    out = dict(first_inputs(seed))
    for name, value in second_inputs(seed + 1).items():
        if name != "x":
            out[name + "_2"] = value
    return out


def reference(
    x, ln1, w_in, conv_w, conv_b, igate_b, fgate_b, mlstm_norm, moba_q_norm, moba_k_norm,
    swa_q_norm, swa_k_norm, swa_sinks, w_out, ln2, w_up, w_down, ffn1_norm_2, ffn1_w_gate_2,
    ffn1_w_up_2, ffn1_w_down_2, mix_norm_2, w_in_2, b_gate_2, na_q_norm_2, na_k_norm_2,
    na_rpb_2, sw_q_norm_2, sw_k_norm_2, sw_sink_2, t5_rel_table_2, w_branch_na_2, w_branch_sw_2,
    w_out_2, ffn2_norm_2, ffn2_w_gate_2, ffn2_w_up_2, ffn2_w_down_2,
):
    x = first_block(
        x, ln1, w_in, conv_w, conv_b, igate_b, fgate_b, mlstm_norm, moba_q_norm, moba_k_norm,
        swa_q_norm, swa_k_norm, swa_sinks, w_out, ln2, w_up, w_down,
    )
    return second_block(
        x, ffn1_norm_2, ffn1_w_gate_2, ffn1_w_up_2, ffn1_w_down_2, mix_norm_2, w_in_2, b_gate_2,
        na_q_norm_2, na_k_norm_2, na_rpb_2, sw_q_norm_2, sw_k_norm_2, sw_sink_2, t5_rel_table_2,
        w_branch_na_2, w_branch_sw_2, w_out_2, ffn2_norm_2, ffn2_w_gate_2, ffn2_w_up_2,
        ffn2_w_down_2,
    )


_drawn_inputs = setup_inputs


def setup_inputs(seed=0):
    import zlib

    import numpy as np

    out = dict(_drawn_inputs(seed))
    spreads = {}
    factors = {'conv_b': 4.1,
     'igate_b': 8.0,
     'mlstm_norm': 4.509,
     'moba_q_norm': 8.0,
     'moba_k_norm': 8.0,
     'swa_q_norm': 8.0,
     'swa_k_norm': 8.0,
     'swa_sinks': 3.648,
     'ffn1_norm_2': 4.041,
     'mix_norm_2': 4.414,
     'b_gate_2': 8.0,
     'na_q_norm_2': 8.0,
     'na_k_norm_2': 8.0,
     'na_rpb_2': 8.0,
     'sw_q_norm_2': 8.0,
     'sw_k_norm_2': 8.0,
     'sw_sink_2': 8.0,
     't5_rel_table_2': 8.0,
     'ffn2_norm_2': 4.126}
    for name, (base, spread) in spreads.items():
        noise = np.random.default_rng([zlib.crc32(name.encode()), seed]).standard_normal(out[name].shape)
        drawn = base * np.exp(spread * noise) if base else spread * noise
        out[name] = __import__('jax').numpy.asarray(drawn.astype(out[name].dtype))
    for name, factor in factors.items():
        out[name] = (out[name] * factor).astype(out[name].dtype)
    return out
```

```python
from contextlib import ExitStack

import numpy as np

import concourse.bass as bass
from concourse import mybir
from concourse.alu_op_type import AluOpType as ALU

F32 = mybir.dt.float32
F32R = mybir.dt.float32r
ACT = mybir.ActivationFunctionType
X = mybir.AxisListType.X

P = 128
S = 256
T = S // P
D = 1024
DC = D // P
DEPTH = 2
HD = 64
EPS = 1e-6
NEG = -1e30
LOWEST = -3.0e38

FF1 = 4 * D
MOBA, LSTM, SWA, SWA_KV = 6, 4, 6, 2
WINDOW1 = 128
TAPS = 4
IN1 = 3 * MOBA * HD + (SWA + 2 * SWA_KV) * HD + 4 * LSTM * HD + 2 * LSTM
PARTS1 = (("mq", MOBA * HD), ("mk", MOBA * HD), ("mv", MOBA * HD), ("sq", SWA * HD), ("sk", SWA_KV * HD),
          ("sv", SWA_KV * HD), ("xqk", 2 * LSTM * HD), ("xv", LSTM * HD), ("xo", LSTM * HD), ("xi", LSTM), ("xf", LSTM))
ORDER1 = ("mq", "sq", "mk", "sk", "xqk", "xi", "xf", "mv", "sv", "xv", "xo")
WIDTH1 = dict(PARTS1)
ZXQK, ZXI, ZXF, ZMV, ZSV, ZXV, ZXO = (sum(WIDTH1[m] for m in ORDER1[:ORDER1.index(n)])
                                      for n in ("xqk", "xi", "xf", "mv", "sv", "xv", "xo"))
QK1 = 2 * MOBA + SWA + SWA_KV
GRID_W = 64
GRID_H = S // GRID_W
NA, SW, SW_KV = 8, 8, 2
NA_ROWS, NA_COLS = 8, 16
RPB_H, RPB_W = 2 * NA_ROWS - 1, 2 * NA_COLS - 1
WINDOW2 = 128
BUCKETS, MAX_DIST = 32, 128
FF2 = 2816
NAW, SWQW, SWKVW = NA * HD, SW * HD, SW_KV * HD
IN2 = 3 * NAW + SWQW + 2 * SWKVW + 2 * D
ZQA, ZKA, ZVA = 0, NAW, 2 * NAW
ZQS = 3 * NAW
ZKS = ZQS + SWQW
ZVS = ZKS + SWKVW
ZG = ZVS + SWKVW
REL = 2 * S

SWA_ORDER = [h + k * (SWA // SWA_KV) for h in range(SWA // SWA_KV) for k in range(SWA_KV)]
SW_ORDER = [h + k * (SW // SW_KV) for h in range(SW // SW_KV) for k in range(SW_KV)]

HALF = 1024
SLAB = 2 * HALF
RAW, RING = 3, 4
PROBS = 4
AHEAD = 3
GROUP = 512

C_LN1, C_LN2, C_CONV, C_CONVB, C_IB, C_FB, C1 = 0, 8, 16, 32, 36, 37, 38
R_GAIN, R_MN, R_SINK, R1 = 0, 256, 512, 518
C2 = 3 * DC
R2_BG, R2_GAIN, R2_SINK, R2 = 0, 2048, 2304, 2312


def groups(width):
    return [(c, min(GROUP, width - c)) for c in range(0, width, GROUP)]


def by_columns(name, rows, c0, w):
    chunks = rows // P
    n = HALF // w
    while chunks % n or (chunks // n) % 2 and chunks // n > 1:
        n -= 1
    return [(name, list(range(k, k + n)), c0, w) for k in range(0, chunks, n)]


def by_rows(name, order):
    return [(name, [k], 0, D) for k in order]


IN2_GROUPS = groups(ZG) + [(ZG + c, w) for c, w in groups(2 * D)]
OUT_ORDER = [0, 1, 2, 5, 6, 7, 3, 4]


def plan1():
    plan = []
    for c0, w in groups(IN1):
        plan += by_columns("w_in", D, c0, w)
    plan += by_rows("w_out", OUT_ORDER)
    for c0, w in groups(FF1):
        plan += by_columns("w_up", D, c0, w)
    return plan + by_rows("w_down", range(FF1 // P))


def plan2():
    plan = []

    def ffn(n):
        for c0, w in groups(FF2):
            plan.extend(by_columns(f"ffn{n}_w_gate_2", D, c0, w))
            plan.extend(by_columns(f"ffn{n}_w_up_2", D, c0, w))
        plan.extend(by_rows(f"ffn{n}_w_down_2", range(FF2 // P)))

    ffn(1)
    for c0, w in IN2_GROUPS:
        plan.extend(by_columns("w_in_2", D, c0, w))
    for c0, w in groups(D):
        plan.extend(by_columns("w_branch_na_2", NAW, c0, w))
        plan.extend(by_columns("w_branch_sw_2", SWQW, c0, w))
    plan.extend(by_rows("w_out_2", range(DC)))
    ffn(2)
    return plan


PLAN1, PLAN2 = plan1(), plan2()
SLABS1, SLABS2 = len(PLAN1) // 2, len(PLAN2) // 2
USES1 = [len(range(s, SLABS1, RAW)) for s in range(RAW)]
USES2 = [len(range(s, SLABS2, RAW)) for s in range(RAW)]


class Book:

    def __init__(self):
        self.unit = 0
        self.made = 0
        self.fills = {}
        self.release = {}
        self.turns = 0
        self.marks = {}

    def fill(self, bank, released_by=None):
        n = self.fills[bank] = self.fills.get(bank, 0) + 1
        before = self.release.get(bank)
        self.release[bank] = released_by
        return n, before

    def mark(self, name, n=1):
        self.marks[name] = self.marks.get(name, 0) + n
        return self.marks[name]


def build(nc, a, out):
    ctx = ExitStack()
    with ctx:
        at = [-(-nc.sbuf_base // 64) * 64]

        def sb(name, shape, dt=F32, offset=None):
            size = 4 * int(np.prod(shape[1:]))
            if offset is None:
                offset = at[0]
                at[0] += -(-size // 32) * 32
            return nc.alloc_sbuf_tensor_at(name, shape, dt, offset=offset)

        def sem(name):
            return ctx.enter_context(nc.semaphore(name))

        x = sb("x_res", [P, T, D])
        work = sb("work", [P, 2048])
        a_hi = sb("a_hi", [P, DC, S], F32R)
        a_lo = sb("a_lo", [P, DC, S], F32R)
        raw = [sb(f"raw{i}", [P, SLAB]) for i in range(RAW)]
        w_hi = [sb(f"w_hi{i}", [P, HALF], F32R) for i in range(RING)]
        w_lo = [sb(f"w_lo{i}", [P, HALF], F32R) for i in range(RING)]
        hidden0 = at[0]
        h_hi = sb("h_hi", [P, FF1 // P, S], F32R)
        h_lo = sb("h_lo", [P, FF1 // P, S], F32R)
        act0 = at[0]
        act_out = [sb(f"act_out{i}", [P, T, GROUP]) for i in range(2)]
        silu0 = at[0]
        silu_out = sb("silu_out", [P, T, GROUP])
        ident = sb("ident", [P, P])
        mask_n = sb("mask_n", [P, S])
        onehot = sb("onehot", [BUCKETS + 1, REL])
        t5_tab = sb("t5_tab", [BUCKETS + 1, SW])
        t5_bias0 = at[0]
        t5_bias = sb("t5_bias", [P, T, SW, S])
        pcol1 = sb("pcol1", [P, DEPTH, C1])
        pcol2 = sb("pcol2", [P, DEPTH, C2])
        pcol = sb("pcol", [P, C1])
        prow = sb("prow", [P, R2])
        half = sb("neg_half", [P, 64])
        ssq = sb("ssq", [P, 64])
        msq = sb("msq", [P, 64])
        rstd_h = sb("rstd_h", [P, 64])
        ss2 = sb("ss2", [P, T])
        ms2 = sb("ms2", [P, T])
        rstd = sb("rstd", [P, T])
        mx = sb("mx", [P, PROBS, T])
        nmx = sb("nmx", [P, PROBS, T])
        esum = sb("esum", [P, PROBS, T])
        esink = sb("esink", [P, PROBS, T])
        tot = sb("tot", [P, PROBS, T])
        rinv = sb("rinv", [P, PROBS, T])
        gcol = sb("gcol", [P, T, 2, LSTM])
        floor = sb("floor", [P, T, LSTM])
        den = sb("den", [P, T, LSTM])
        dabs = sb("dabs", [P, T, LSTM])
        drec = sb("drec", [P, T, LSTM])
        assert at[0] <= nc.sbuf_usable_end, (at[0], nc.sbuf_usable_end)

        o = [hidden0]

        def over(name, shape):
            t = sb(name, shape, offset=o[0])
            o[0] += 4 * int(np.prod(shape[1:]))
            return t

        z1 = over("z1", [P, T, IN1])
        qk = over("qk", [P, T, QK1 * HD])
        kz1 = over("keys_t1", [P, 6, 2, S])
        hT1 = over("heads_t1", [P, 10, S])
        xT = over("conv_in", [P, 4, S])
        gates = [over(f"gate{i}", [LSTM, S]) for i in range(3)]
        assert o[0] <= hidden0 + 8 * FF1 // P * S
        o[0] = hidden0
        z2 = over("z2", [P, T, IN2])
        na_bias = over("na_bias", [P, T, NA, S])
        hT2 = over("heads_t2", [P, 8, S])
        probT2 = over("prob_t2", [P, 2 * GROUP])
        assert o[0] <= hidden0 + 8 * FF1 // P * S
        sq2_at = hidden0 + 4 * (T * IN2 + T * NA * S)
        sq2 = sb("sq2", [P, T, 26 * HD], offset=sq2_at)
        gain2 = sb("gain2", [P, 4, HD], offset=sq2_at + 4 * T * 26 * HD)
        assert sq2_at + 4 * (T * 26 * HD + 4 * HD) <= hidden0 + 8 * FF1 // P * S
        kz2 = sb("keys_t2", [P, 5, 2, S], offset=act0)
        qk_b = sb("qk_b", [P, T, QK1 * HD], offset=hidden0 + 4 * T * (IN1 + QK1 * HD))
        sq1 = sb("sq1", [P, T, QK1 * HD], offset=hidden0 + 4 * (T * (IN1 + QK1 * HD) + 12 * S))
        o[0] = t5_bias0
        rope_c = over("rope_c", [P, T, 4, HD])
        rope_s = over("rope_s", [P, T, 4, HD])
        mask_m = over("mask_m", [P, 3 * P])
        mask_s = over("mask_s", [P, 3 * P])
        pick = over("pick", [LSTM, LSTM, P])
        ones = over("ones", [LSTM, S])
        g_row = over("g_row", [LSTM, 2, S])
        g_u = over("g_u", [LSTM, S])
        assert o[0] <= t5_bias0 + 4 * T * SW * S
        g_in, g_f, g_e = gates
        g_cum, g_m = g_e, g_f
        lstm_h = sb("lstm_h", [P, T, LSTM * HD], offset=hidden0 + 4 * T * IN1)
        lstm_q = sb("lstm_q", [P, T, LSTM * HD], offset=hidden0 + 4 * T * (IN1 + QK1 * HD))
        t5_rel = sb("t5_rel", [SW, REL], offset=silu0)

        prob = [work[:, i * GROUP:(i + 1) * GROUP] for i in range(PROBS)]
        probT1 = silu_out[:, :, :].rearrange("p t n -> p (t n)")
        rope_gc = act_out[0][:, :, :].rearrange("p t (y d) -> p t y d", d=HD)[:, :, 0:4, :]
        rope_gs = act_out[1][:, :, :].rearrange("p t (y d) -> p t y d", d=HD)[:, :, 0:4, :]

        acc = [ctx.enter_context(nc.psum_tensor(f"acc{i}", [P, GROUP], F32)) for i in range(4)]
        sc = [ctx.enter_context(nc.psum_tensor(f"sc{i}", [P, GROUP], F32)) for i in range(2)]
        tp = [ctx.enter_context(nc.psum_tensor(f"tp{i}", [P, GROUP], F32)) for i in range(2)]

        const_in = sem("const_in")
        x_in = sem("x_in")
        t5_dram = nc.dram_tensor("t5_by_distance", [SW, REL], F32).ap()
        na_skew = nc.dram_tensor("na_skew", [DEPTH, P, T, NA, S], F32).ap()
        skewed = sem("na_skewed")
        slab_in = [sem(f"slab_in{i}") for i in range(RAW)]
        slab_free = sem("slab_free")
        streamed = sem("layer_streamed")
        t5_read = sem("t5_read")
        t5_row = sem("t5_row")
        t5_out = sem("t5_out")
        t5_turned = sem("t5_turned")
        t5_skew = nc.dram_tensor("t5_skew", [P, T, SW, S], F32).ap()
        t5_in = sem("t5_in")
        base_in = sem("base_in")
        x_final = sem("x_final")
        stored = sem("stored")
        go = {e: sem(f"go_{e}") for e in ("act", "dve", "pe")}

        first_stage = sem("layer_done")
        layer_done = first_stage
        names = """act_chain dve_chain pool_chain unit_hi unit_lo units_used
            tp_full0 tp_full1 acc_full0 acc_full1 acc_full2 acc_full3 sc_full0 sc_full1
            cols_ready rows_in ssx_ready msx_ready rstd_ready turn_hi turn_lo x_new
            z_act z_dve relu_out act_ready hid_hi hid_lo silu_done
            sq_ready ms_ready rsh_ready tables_ready normed rope_a_ready rope_b_ready qk_ready conv_seen gates_seen
            gate_abs gate_ln gate_rows gcol_ready floor_ready conv_done silu_conv xo_ready heads_t
            kz_ready score_seen d_seen shift_ready exp_done esum_ready prob_ready probT_ready pair_hi pair_lo
            lstm_seen y_ready bias_in bias_ready g_ready na_out sw_out merged lsq_ready""".split()
        s = {n: sem(n) for n in names}
        nums = [v.num for v in [layer_done, *s.values()]]
        assert sorted(nums) == list(range(min(nums), min(nums) + len(nums)))
        tp_full = [s["tp_full0"], s["tp_full1"]]
        acc_full = [s[f"acc_full{i}"] for i in range(4)]
        sc_full = [s["sc_full0"], s["sc_full1"]]
        act_chain, dve_chain, pool_chain = s["act_chain"], s["dve_chain"], s["pool_chain"]

        def wait(eng, what):
            if what is not None:
                eng.wait_ge(what[0], what[1])

        def tick(eng, b, chain, ins):
            ins.then_inc(chain, 1)
            eng.wait_ge(chain, b.mark("chain"))


        def act_split(act, b, l, plan, slabs1, uses, to):
            while b.made < min(to, len(plan)):
                u = b.made
                name, chunks, c0, w = plan[u]
                n = len(chunks) * w
                j, slot = u // 2, (u // 2) % RAW
                if u % 2 == 0:
                    base = slabs1[slot]
                    act.wait_ge(slab_in[slot], (l * uses[slot] + base + j // RAW + 1) * 16)
                if u >= RING:
                    act.wait_ge(s["units_used"], u - RING + 1)
                nc.scalar.activation(w_hi[u % RING][:, 0:n], raw[slot][:, (u % 2) * HALF:(u % 2) * HALF + n],
                                     ACT.Copy).then_inc(s["unit_hi"], 1)
                b.made += 1

        def dve_split(dve, b, plan, to):
            while b.made < min(to, len(plan)):
                u = b.made
                name, chunks, c0, w = plan[u]
                n = len(chunks) * w
                slot = (u // 2) % RAW
                dve.wait_ge(s["unit_hi"], u + 1)
                nc.vector.tensor_tensor(w_lo[u % RING][:, 0:n], raw[slot][:, (u % 2) * HALF:(u % 2) * HALF + n],
                                        w_hi[u % RING][:, 0:n].bitcast(F32), ALU.subtract).then_inc(s["unit_lo"], 1)
                b.made += 1
                if u % 2:
                    dve.wait_ge(s["unit_lo"], u + 1)
                    dve.sem_inc(slab_free, 1)

        def pe_unit(pe, b, plan, hi, lo, banks, first, last, shift):
            u = b.unit
            name, chunks, c0, w = plan[u]
            pe.wait_ge(s["unit_lo"], u + 1)
            cols = min(w, GROUP)
            for i, c in enumerate(chunks):
                for t in range(T):
                    for n in range(w // cols):
                        o_ = banks[t * (w // cols) + n][:, 0:cols]
                        col = slice(i * w + n * cols, i * w + (n + 1) * cols)
                        xh, xl = hi[:, c + shift, t * P:(t + 1) * P], lo[:, c + shift, t * P:(t + 1) * P]
                        wh, wl = w_hi[u % RING][:, col], w_lo[u % RING][:, col]
                        nc.tensor.matmul(o_, xh, wh, start=first and i == 0, stop=False)
                        nc.tensor.matmul(o_, xh, wl, start=False, stop=False)
                        mm = nc.tensor.matmul(o_, xl, wh, start=False, stop=last and i == len(chunks) - 1)
                        if last and i == len(chunks) - 1 and not (t == T - 1 and n == w // cols - 1):
                            mm.then_inc(acc_full[acc.index(banks[t * (w // cols) + n])], 1)
            b.unit += 1
            return mm

        def pe_stream(pe, b, plan, n_units, hi, lo, banks, released_by, need=None, shift=0):
            for k, i in enumerate(banks):
                _, before = b.fill(("acc", i), released_by[k])
                wait(pe, before)
            for n in range(n_units):
                if need is not None:
                    wait(pe, need(n))
                mm = pe_unit(pe, b, plan, hi, lo, [acc[i] for i in banks], n == 0, n == n_units - 1, shift)
                mm.then_inc(s["units_used"], 1)
            for i in banks[:-1]:
                b.mark(f"acc_full{i}")

        def stream_done(b, banks, n_units):
            b.unit += n_units
            return [(acc_full[i], b.mark(f"acc_full{i}")) for i in banks[:-1]] + [(s["units_used"], b.unit)]

        def turn_fills(b):
            for f in range(DC // 2):
                b.turns += 1
                q = b.mark("tp") - 1
                bank = q % 2
                n, before = b.fill(("tp", bank), (s["turn_lo"], b.turns))
                yield f, bank, n, before, b.turns

        def pe_turn(pe, b, src, need):
            for f, bank, n, before, k in turn_fills(b):
                wait(pe, need(f))
                wait(pe, before)
                for i in range(2):
                    for t in range(T):
                        c = 2 * f + i
                        mm = nc.tensor.transpose(tp[bank][:, i * S + t * P:i * S + (t + 1) * P],
                                                 src(t, c), ident[:, :])
                mm.then_inc(tp_full[bank], 1)

        def act_turn(act, b, gain):
            for f, bank, n, before, k in turn_fills(b):
                act.wait_ge(tp_full[bank], n)
                for i in range(2):
                    c = 2 * f + i
                    g = 1.0 if gain is None else pcol[:, gain + c:gain + c + 1]
                    ins = nc.scalar.activation(a_hi[:, c, :], tp[bank][:, i * S:(i + 1) * S], ACT.Identity, scale=g)
                ins.then_inc(s["turn_hi"], 1)

        def dve_turn(dve, b, gain):
            for f, bank, n, before, k in turn_fills(b):
                dve.wait_ge(s["turn_hi"], k)
                for i in range(2):
                    c = 2 * f + i
                    g = 1.0 if gain is None else pcol[:, gain + c:gain + c + 1]
                    ins = nc.vector.scalar_tensor_tensor(out=a_lo[:, c, :], in0=tp[bank][:, i * S:(i + 1) * S],
                                                         scalar=g, in1=a_hi[:, c, :].bitcast(F32),
                                                         op0=ALU.mult, op1=ALU.subtract)
                ins.then_inc(s["turn_lo"], 1)

        def act_norm(act, b, need):
            wait(act, need)
            for t in range(T):
                ins = nc.scalar.activation(work[:, t * D:(t + 1) * D], x[:, t, :], ACT.Square,
                                           accum_out=ss2[:, t:t + 1])
            ins.then_inc(s["ssx_ready"], 1)
            b.mark("norm")

        def dve_norm(dve, b):
            n = b.mark("norm")
            dve.wait_ge(s["ssx_ready"], n)
            nc.vector.tensor_scalar(ms2[:, :], ss2[:, :], 1.0 / D, EPS, ALU.mult, ALU.add).then_inc(s["msx_ready"], 1)

        def zero_halves(kz):
            nc.gpsimd.memset(kz[HD:P, :, 0, :], 0.0)
            nc.gpsimd.memset(kz[0:HD, :, 1, :], 0.0).then_inc(s["kz_ready"], 1)

        def pool_norm(pool, b):
            n = b.mark("norm")
            pool.wait_ge(s["msx_ready"], n)
            nc.gpsimd.tensor_tensor(rstd[:, :], ms2[:, :], half[:, 0:T], ALU.pow).then_inc(s["rstd_ready"], 1)

        def dve_add_x(dve, b, scale, n_units):
            full = stream_done(b, range(4), n_units)
            for n in range(2):
                for t in range(T):
                    i = 2 * t + n
                    wait(dve, full[i])
                    xs = x[:, t, n * GROUP:(n + 1) * GROUP]
                    nc.vector.scalar_tensor_tensor(out=xs, in0=acc[i][:, :], scalar=scale, in1=xs, op0=ALU.mult,
                                                   op1=ALU.add).then_inc(s["x_new"], 1)
                    b.mark("x_new")

        def released_x(b):
            m = b.marks.get("x_new", 0)
            return [(s["x_new"], m + 1 + 2 * (i % 2) + i // 2) for i in range(4)]

        def layer_end(eng, name, b):
            eng.sem_inc(layer_done, 1)
            eng.wait_ge(go[name], 1)
            eng.sem_clear(go[name])

        blk = ctx.enter_context(nc.Block())
        BASE = (("pcol1", pcol1), ("ident", ident), ("neg_half", half))
        CONSTS = ((pcol2, "pcol2"), (rope_c, "rope_c"), (rope_s, "rope_s"), (mask_m, "mask_m"), (mask_s, "mask_s"),
                  (pick, "pick"), (mask_n, "mask_n"), (ones, "ones"), (onehot, "onehot"))
        n_const = len(CONSTS) + 2
        STAGES = 4

        @blk.sync
        def _(sp):
            x_tiles = a["x"].rearrange("o (t p) d -> p (o t) d", p=P)
            for name, dst in BASE:
                sp.dma_start(dst[:], a[name]).then_inc(base_in, 16)
            for t in range(T):
                sp.dma_start(x[:, t, :], x_tiles[:, t, :]).then_inc(x_in, 16)
            for k in range(RAW):
                sp.dma_start(raw[k][:, :], a["slabs1"][k]).then_inc(slab_in[k], 16)
            for dst, name in CONSTS:
                sp.dma_start(dst[:], a[name]).then_inc(const_in, 16)
            sp.dma_start(t5_tab[0:BUCKETS, :], a["t5_rel_table_2"]).then_inc(const_in, 16)
            sp.dma_start(t5_tab[BUCKETS:BUCKETS + 1, :], a["ones"][0:1, 0:SW]).then_inc(const_in, 16)
            rounds = DEPTH * SLABS1 // RAW
            for stage in range(STAGES):
                with sp.Fori(1 + (rounds - 1) * stage // STAGES, 1 + (rounds - 1) * (stage + 1) // STAGES) as i:
                    for k in range(RAW):
                        src = a["slabs1"][bass.ds(i * RAW + k, 1)].rearrange("o p n -> (o p) n")
                        sp.wait_ge(slab_free, i * RAW + (k + 1 - RAW))
                        sp.dma_start(raw[k][:, :], src).then_inc(slab_in[k], 16)
                for lr in range(stage * DEPTH * GRID_H // STAGES, (stage + 1) * DEPTH * GRID_H // STAGES):
                    l, r = lr // GRID_H, lr % GRID_H
                    t, i = r // 2, r % 2
                    for kr in range(GRID_H):
                        row = (NA_ROWS - 1 - r + kr) * RPB_W + NA_COLS - 1
                        src = bass.AP(a["rpb"].tensor, l * (NA * RPB_H * RPB_W) + row,
                                      [[RPB_H * RPB_W, NA], [-1, GRID_W], [1, GRID_W]])
                        dst = na_skew[l, i * GRID_W:(i + 1) * GRID_W, t, :, kr * GRID_W:(kr + 1) * GRID_W]
                        sp.dma_start(dst.rearrange("p h k -> h p k"), src).then_inc(skewed, 16)
            done = DEPTH * SLABS1
            whole = SLABS2 // RAW
            with sp.Fori(0, DEPTH) as l:
                with sp.Fori(0, whole) as i:
                    for k in range(RAW):
                        src = a["slabs2"][bass.ds(l * SLABS2 + i * RAW + k, 1)].rearrange("o p n -> (o p) n")
                        sp.wait_ge(slab_free, l * SLABS2 + i * RAW + (done + k + 1 - RAW))
                        sp.dma_start(raw[k][:, :], src).then_inc(slab_in[k], 16)
                for k in range(SLABS2 - RAW * whole):
                    src = a["slabs2"][bass.ds(l * SLABS2 + (RAW * whole + k), 1)].rearrange("o p n -> (o p) n")
                    sp.wait_ge(slab_free, l * SLABS2 + (done + RAW * whole + k + 1 - RAW))
                    sp.dma_start(raw[k][:, :], src).then_inc(slab_in[k], 16)
                sp.wait_ge(slab_free, l * SLABS2 + (done + SLABS2))
                sp.sem_inc(streamed, 1)
            sp.wait_ge(x_final, 1)
            sp.dma_start(out.rearrange("o (t p) d -> p (o t) d", p=P), x[:, :, :]).then_inc(stored, 16)
            sp.wait_ge(stored, 16)

        QK_GROUP = (QK1 * HD - 1) // GROUP
        CONV_AFTER = (ZXF + LSTM - 1) // GROUP + 1

        def pe_layer1(pe):
            b = Book()
            pe_turn(pe, b, lambda t, c: x[:, t, c * P:(c + 1) * P], lambda f: None)
            for g, (c0, w) in enumerate(groups(IN1)):
                pe_stream(pe, b, PLAN1, len(by_columns("", D, c0, w)), a_hi, a_lo,
                          [2 * (g % 2), 2 * (g % 2) + 1], [(s["z_act"], 2 * g + 1), (s["z_act"], 2 * g + 2)],
                          lambda n: (s["turn_lo"], b.turns) if g == 0 and n == 0 else None)
                if g != CONV_AFTER:
                    continue
                pe.wait_ge(s["z_act"], 2 * CONV_AFTER)
                for f in range(2):
                    bank, n, before = conv_fill(b)
                    wait(pe, before)
                    for i in range(2):
                        for t in range(T):
                            c = ZXQK + (2 * f + i) * P
                            mm = nc.tensor.transpose(tp[bank][:, i * S + t * P:i * S + (t + 1) * P],
                                                     z1[:, t, c:c + P], ident[:, :])
                    mm.then_inc(tp_full[bank], 1)
                bank, n, before = gate_fill(b)
                wait(pe, before)
                for i, c in enumerate((ZXI, ZXF)):
                    for t in range(T):
                        mm = nc.tensor.transpose(tp[bank][0:LSTM, i * S + t * P:i * S + (t + 1) * P],
                                                 z1[:, t, c:c + LSTM], ident[:, :])
                mm.then_inc(tp_full[bank], 1)
            pe.wait_ge(s["z_act"], 2 * len(groups(IN1)))
            pe.wait_ge(s["qk_ready"], 1)
            for f in range(5):
                bank, n, before = heads_fill(b)
                wait(pe, before)
                for i in range(2):
                    for t in range(T):
                        c = (2 * f + i) * P
                        mm = nc.tensor.transpose(tp[bank][:, i * S + t * P:i * S + (t + 1) * P],
                                                 qk[:, t, c:c + P], ident[:, :])
                mm.then_inc(tp_full[bank], 1)
            bank, n, before = gcol_fill(b)
            wait(pe, before)
            pe.wait_ge(s["gate_rows"], 1)
            for t in range(T):
                for i in range(2):
                    c = (2 * t + i) * LSTM
                    mm = nc.tensor.transpose(tp[bank][:, c:c + LSTM], g_row[:, i, t * P:(t + 1) * P],
                                             ident[0:LSTM, 0:LSTM])
            mm.then_inc(tp_full[bank], 1)
            pe_heads(pe, b, HEADS1)
            pe.wait_ge(s["y_ready"], 1)
            bank, n, before, k = y_fill(b)
            wait(pe, before)
            for i in range(2):
                for t in range(T):
                    mm = nc.tensor.transpose(tp[bank][:, i * S + t * P:i * S + (t + 1) * P],
                                             lstm_h[:, t, i * P:(i + 1) * P], ident[:, :])
            mm.then_inc(tp_full[bank], 1)
            pe_stream(pe, b, PLAN1, DC, a_hi, a_lo, range(4), released_x(b),
                      lambda n: (s["pair_lo"], min(n, 6) + 1))
            b.mark("x_new", 4)
            xn = b.marks["x_new"]
            pe_turn(pe, b, lambda t, c: x[:, t, c * P:(c + 1) * P],
                    lambda f: (s["x_new"], xn - 2 + 2 * (f // 2)))
            gs = groups(FF1)
            for g, (c0, w) in enumerate(gs):
                pe_stream(pe, b, PLAN1, len(by_columns("", D, c0, w)), a_hi, a_lo,
                          [2 * (g % 2), 2 * (g % 2) + 1], [(s["relu_out"], g + 1)] * 2,
                          lambda n: (s["turn_lo"], b.turns) if g == 0 and n == 0 else None)
                if g:
                    pe_hidden(pe, b, g - 1, gs[g - 1][1])
            pe_hidden(pe, b, len(gs) - 1, gs[-1][1])
            pe_stream(pe, b, PLAN1, FF1 // P, h_hi, h_lo, range(4), released_x(b),
                      lambda n: (s["hid_lo"], n // 2 + 1) if n % 2 == 0 else None)
            b.mark("x_new", 4)
            pe.wait_ge(s["units_used"], b.unit)
            layer_end(pe, "pe", b)

        def hidden_fills(b, width):
            for f in range(width // (2 * P)):
                k = b.mark("hid")
                q = b.mark("tp") - 1
                bank = q % 2
                n, before = b.fill(("tp", bank), (s["hid_lo"], k))
                yield f, bank, n, before, k

        def pe_hidden(pe, b, g, width):
            pe.wait_ge(s["act_ready"], b.mark("act_ready"))
            for f, bank, n, before, k in hidden_fills(b, width):
                wait(pe, before)
                for i in range(2):
                    for t in range(T):
                        c = (2 * f + i) * P
                        mm = nc.tensor.transpose(tp[bank][:, i * S + t * P:i * S + (t + 1) * P],
                                                 act_out[g % 2][:, t, c:c + P], ident[:, :])
                mm.then_inc(tp_full[bank], 1)

        def act_hidden(act, b, g, width):
            for f, bank, n, before, k in hidden_fills(b, width):
                act.wait_ge(tp_full[bank], n)
                c = g * (GROUP // P) + 2 * f
                nc.scalar.activation(h_hi[:, c:c + 2, :], tp[bank][:, :].rearrange("p (c s) -> p c s", s=S),
                                     ACT.Copy).then_inc(s["hid_hi"], 1)

        def dve_hidden(dve, b, g, width):
            for f, bank, n, before, k in hidden_fills(b, width):
                dve.wait_ge(s["hid_hi"], k)
                c = g * (GROUP // P) + 2 * f
                nc.vector.tensor_tensor(h_lo[:, c:c + 2, :], tp[bank][:, :].rearrange("p (c s) -> p c s", s=S),
                                        h_hi[:, c:c + 2, :].bitcast(F32), ALU.subtract).then_inc(s["hid_lo"], 1)

        def next_tp(b, released_by):
            q = b.mark("tp") - 1
            bank = q % 2
            n, before = b.fill(("tp", bank), released_by)
            return bank, n, before

        def conv_fill(b):
            return next_tp(b, (s["conv_seen"], b.mark("conv")))

        def gate_fill(b):
            return next_tp(b, (s["gates_seen"], 1))

        def heads_fill(b):
            return next_tp(b, (s["heads_t"], b.mark("heads")))

        def gcol_fill(b):
            return next_tp(b, (s["gcol_ready"], 1))

        def y_fill(b):
            k = b.mark("pair")
            return (*next_tp(b, (s["pair_lo"], k)), k)

        HEADS1 = []
        for h in range(MOBA):
            HEADS1.append(dict(kind="soft", q=h // 2, k=h // 2, half=h % 2, v=ZMV + h * HD, sink=None,
                               chunk=h // 2, mask=mask_m))
        for i, h in enumerate(SWA_ORDER):
            HEADS1.append(dict(kind="soft", q=3 + i // 2, k=3, half=i % 2, v=ZSV + (i % 2) * HD, sink=h,
                               chunk=5 + i // 2, mask=mask_s))
        for h in range(LSTM):
            HEADS1.append(dict(kind="lstm", q=6 + h // 2, k=4 + h // 2, half=h % 2, v=ZXV + h * HD, h=h))
        HEADS2 = []
        for h in range(NA):
            HEADS2.append(dict(kind="full", q=h // 2, k=h // 2, half=h % 2, v=ZVA + h * HD, sink=None,
                               chunk=h // 2, bias=na_bias, h=h))
        for i, h in enumerate(SW_ORDER):
            HEADS2.append(dict(kind="full", q=4 + i // 2, k=4, half=i % 2, v=ZVS + (i % 2) * HD, sink=h,
                               chunk=4 + i // 2, bias=t5_bias, h=h))

        def head_fills(b, heads):
            soft = [i for i, h in enumerate(heads) if h["kind"] != "lstm"]
            plan = []
            for i, h in enumerate(heads):
                e = {}
                rel = (s["prob_ready" if h["kind"] == "lstm" else "score_seen"], i + 1)
                e["sc"] = (i % 2, *b.fill(("sc", i % 2), rel))
                e["tp"] = next_tp(b, (s["probT_ready"], i + 1))
                if h["kind"] == "lstm":
                    m = h["h"]
                    _, before = b.fill(("acc", m % 2), (s["d_seen"], m + 1))
                    e["d"] = (m % 2, b.mark(f"acc_full{m % 2}"), before)
                    if m == 0:
                        _, before = b.fill(("acc", 2), (s["lstm_seen"], 1))
                        e["o"] = (2, b.mark("acc_full2"), before)
                    else:
                        e["o"] = plan[-1]["o"]
                elif i % 2 == 0:
                    pair = b.mark("pair")
                    bank = 2 + (pair - 1) % 2
                    _, before = b.fill(("acc", bank), (s["pair_lo"], pair))
                    e["o"] = (bank, b.mark(f"acc_full{bank}"), before)
                    e["pair"] = pair
                else:
                    e["o"] = plan[-1]["o"]
                    e["pair"] = plan[-1]["pair"]
                plan.append(e)
            return plan

        def pe_heads(pe, b, heads):
            fills = head_fills(b, heads)
            hT, kz, probT = (hT1, kz1, probT1) if heads is HEADS1 else (hT2, kz2, probT2)
            z = z1 if heads is HEADS1 else z2
            full = heads is HEADS2
            n = len(heads)

            def scores(i):
                h = heads[i]
                bank, k, before = fills[i]["sc"]
                q, kk = hT[:, h["q"], :], kz[:, h["k"], h["half"], :]
                if i == 0:
                    pe.wait_ge(s["heads_t"], 7 if full else 5)
                    pe.wait_ge(s["kz_ready"], 1)
                if h["kind"] == "lstm":
                    if h["h"] == 0:
                        pe.wait_ge(s["silu_conv"], 1)
                    dbank, dk, dbefore = fills[i]["d"]
                    wait(pe, dbefore)
                    nc.tensor.matmul(acc[dbank][:, 0:P], pick[:, h["h"], :], g_u[:, 0:P], start=True, stop=True)
                    nc.tensor.matmul(acc[dbank][:, P:3 * P], pick[:, h["h"], :], g_u[:, :], start=True,
                                     stop=True).then_inc(acc_full[dbank], 1)
                wait(pe, before)
                if full:
                    nc.tensor.matmul(sc[bank][:, 0:S], q[:, 0:P], kk, start=True, stop=True)
                    nc.tensor.matmul(sc[bank][:, S:2 * S], q[:, P:S], kk, start=True, stop=True)\
                        .then_inc(sc_full[bank], 1)
                else:
                    nc.tensor.matmul(sc[bank][:, 0:P], q[:, 0:P], kk[:, 0:P], start=True, stop=True)
                    nc.tensor.matmul(sc[bank][:, P:3 * P], q[:, P:S], kk, start=True, stop=True)\
                        .then_inc(sc_full[bank], 1)

            def turn(i):
                bank, k, before = fills[i]["tp"]
                pe.wait_ge(s["prob_ready"], i + 1)
                wait(pe, before)
                blocks = 4 if full else 3
                src = prob[i % PROBS]
                for j in range(blocks):
                    frm = (j % 2) * 2 + j // 2 if full else j
                    mm = nc.tensor.transpose(tp[bank][:, j * P:(j + 1) * P], src[:, frm * P:(frm + 1) * P],
                                             ident[:, :])
                mm.then_inc(tp_full[bank], 1)

            def values(i):
                h = heads[i]
                bank, k, before = fills[i]["o"]
                pT = probT[:, (i % 2) * GROUP:(i % 2 + 1) * GROUP]
                pe.wait_ge(s["probT_ready"], i + 1)
                v = [z[:, t, h["v"]:h["v"] + HD] for t in range(T)]
                if h["kind"] == "lstm":
                    m = h["h"]
                    if m == 0:
                        wait(pe, before)
                    ob = acc[bank][:, :].rearrange("p (t h d) -> p t h d", t=T, d=HD)
                    nc.tensor.matmul(ob[:, 0, m, :], pT[:, 0:P], v[0], start=True, stop=True)
                    nc.tensor.matmul(ob[:, 1, m, :], pT[:, P:2 * P], v[0], start=True, stop=False)
                    mm = nc.tensor.matmul(ob[:, 1, m, :], pT[:, 2 * P:3 * P], v[1], start=False, stop=True)
                    if m == LSTM - 1:
                        mm.then_inc(acc_full[bank], 1)
                    return
                if h["half"] == 0:
                    wait(pe, before)
                p0 = h["half"] * HD
                ob = acc[bank][p0:p0 + HD, 0:S]
                if full:
                    nc.tensor.matmul(ob, v[0], pT[:, 0:S], start=True, stop=False)
                    mm = nc.tensor.matmul(ob, v[1], pT[:, S:2 * S], start=False, stop=True)
                else:
                    nc.tensor.matmul(ob, v[0], pT[:, 0:S], start=True, stop=False)
                    mm = nc.tensor.matmul(ob[:, P:S], v[1], pT[:, 2 * P:3 * P], start=False, stop=True)
                if h["half"] == 1:
                    mm.then_inc(acc_full[bank], 1)

            for i in range(PROBS):
                scores(i)
            for i in range(n + 1):
                if i < n:
                    turn(i)
                if i >= 1:
                    values(i - 1)
                if i + PROBS < n:
                    scores(i + PROBS)

        def dve_heads(dve, b, heads):
            fills = head_fills(b, heads)
            full = heads is HEADS2
            n = len(heads)
            tiles = [slice(0, S), slice(S, 2 * S)] if full else [slice(0, P), slice(P, 3 * P)]

            def first(i):
                h, p = heads[i], i % PROBS
                bank, k, before = fills[i]["sc"]
                if i >= PROBS:
                    tb, tk, _ = fills[i - PROBS]["tp"]
                    dve.wait_ge(tp_full[tb], tk)
                if h["kind"] == "lstm":
                    dbank, dk, _ = fills[i]["d"]
                    dve.wait_ge(acc_full[dbank], dk)
                    nc.vector.tensor_tensor(prob[p][:, 0:3 * P], acc[dbank][:, 0:3 * P], mask_m[:, :],
                                            ALU.add).then_inc(s["d_seen"], 1)
                    return
                dve.wait_ge(sc_full[bank], k)
                for t in range(T):
                    extra = h["bias"][:, t, h["h"], :] if full else h["mask"][:, tiles[t]]
                    start = LOWEST if h["sink"] is None else sinks(heads)[:, h["sink"]:h["sink"] + 1]
                    ins = nc.vector.tensor_tensor_reduce(prob[p][:, tiles[t]], sc[bank][:, tiles[t]], extra, 1.0,
                                                         start, ALU.add, ALU.max, mx[:, p, t:t + 1])
                ins.then_inc(s["score_seen"], 1)
                dve.wait_ge(s["score_seen"], i + 1)
                nc.vector.tensor_scalar(nmx[:, p, :], mx[:, p, :], -1.0, None, ALU.mult)\
                    .then_inc(s["shift_ready"], 1)

            def second(i):
                h, p = heads[i], i % PROBS
                dve.wait_ge(s["exp_done"], i + 1)
                if h["kind"] == "lstm":
                    bank, k, before = fills[i]["sc"]
                    dve.wait_ge(sc_full[bank], k)
                    for t in range(T):
                        ins = nc.vector.scalar_tensor_tensor(out=prob[p][:, tiles[t]], in0=sc[bank][:, tiles[t]],
                                                             scalar=HD ** -0.5, in1=prob[p][:, tiles[t]],
                                                             op0=ALU.mult, op1=ALU.mult,
                                                             accum_out=den[:, t, h["h"]:h["h"] + 1])
                    ins.then_inc(s["prob_ready"], 1)
                    return
                total = esum
                if h["sink"] is not None:
                    tick(dve, b, dve_chain, nc.vector.tensor_tensor(tot[:, p, :], esum[:, p, :], esink[:, p, :],
                                                                    ALU.add))
                    total = tot
                tick(dve, b, dve_chain, nc.vector.reciprocal(rinv[:, p, :], total[:, p, :]))
                for t in range(T):
                    ins = nc.vector.tensor_scalar(prob[p][:, tiles[t]], prob[p][:, tiles[t]], rinv[:, p, t:t + 1],
                                                  None, ALU.mult)
                ins.then_inc(s["prob_ready"], 1)

            def pair(i):
                h = heads[i]
                if h["kind"] == "lstm" or h["half"] == 0:
                    return
                bank = fills[i]["o"][0]
                k = fills[i]["pair"]
                dve.wait_ge(s["pair_hi"], k)
                nc.vector.tensor_tensor(a_lo[:, h["chunk"], :], acc[bank][:, 0:S],
                                        a_hi[:, h["chunk"], :].bitcast(F32), ALU.subtract).then_inc(s["pair_lo"], 1)

            for i in range(n + 5):
                if i < n:
                    first(i)
                if 2 <= i < n + 2:
                    second(i - 2)
                if i >= 5:
                    pair(i - 5)

        def sinks(heads):
            r = R_SINK if heads is HEADS1 else R2_SINK
            return prow[:, r:r + 8]

        def act_heads(act, b, heads):
            fills = head_fills(b, heads)
            full = heads is HEADS2
            n = len(heads)
            tiles = [slice(0, S), slice(S, 2 * S)] if full else [slice(0, P), slice(P, 3 * P)]
            used = 2 * S if full else 3 * P
            probT = probT2 if full else probT1

            def exps(i):
                h, p = heads[i], i % PROBS
                if h["kind"] == "lstm":
                    act.wait_ge(s["d_seen"], h["h"] + 1)
                    for t in range(T):
                        m = gcol[:, t, 0, h["h"]:h["h"] + 1]
                        ins = nc.scalar.activation(prob[p][:, tiles[t]], prob[p][:, tiles[t]], ACT.Exp, bias=m)
                    ins.then_inc(s["exp_done"], 1)
                    return
                soft = sum(g["kind"] != "lstm" for g in heads[:i + 1])
                act.wait_ge(s["shift_ready"], soft)
                if h["sink"] is not None:
                    sk = sinks(heads)[:, h["sink"]:h["sink"] + 1]
                    nc.scalar.activation(esink[:, p, :], nmx[:, p, :], ACT.Exp, bias=sk)
                for t in range(T):
                    ins = nc.scalar.activation(prob[p][:, tiles[t]], prob[p][:, tiles[t]], ACT.Exp,
                                               bias=nmx[:, p, t:t + 1], accum_out=esum[:, p, t:t + 1])
                ins.then_inc(s["exp_done"], 1)

            def copy(i):
                bank, k, _ = fills[i]["tp"]
                act.wait_ge(tp_full[bank], k)
                nc.scalar.copy(probT[:, (i % 2) * GROUP:(i % 2) * GROUP + used], tp[bank][:, 0:used]).then_inc(s["probT_ready"], 1)

            def pair(i):
                h = heads[i]
                if h["kind"] == "lstm" or h["half"] == 0:
                    return
                bank, k, _ = fills[i]["o"]
                act.wait_ge(acc_full[bank], k)
                nc.scalar.activation(a_hi[:, h["chunk"], :], acc[bank][:, 0:S], ACT.Copy).then_inc(s["pair_hi"], 1)

            for i in range(n + 5):
                if i < n:
                    exps(i)
                if 3 <= i < n + 3:
                    copy(i - 3)
                if i >= 5:
                    pair(i - 5)

        TYPES1 = ((0, MOBA, 0), (MOBA, SWA, 2), (MOBA + SWA, MOBA, 1), (2 * MOBA + SWA, SWA_KV, 3))
        RUNS2 = ((0, ZQA, 2 * NA), (2 * NA, ZQS, SW + SW_KV))
        TYPES2 = ((ZQA, NA), (ZKA, NA), (ZQS, SW), (ZKS, SW_KV))

        def by_head(t):
            return t.rearrange("p t (h d) -> p t h d", d=HD)

        def base_const(eng):
            eng.wait_ge(x_in, 16 * T)
            eng.wait_ge(base_in, 16 * len(BASE))

        def copy_heads(hT, kz, f, q_fills, src, tiles):
            if f < q_fills:
                return nc.scalar.copy(hT[:, 2 * f:2 * f + 2, :], src[:, :].rearrange("p (c s) -> p c s", s=S))
            j = 2 * (f - q_fills)
            for i in range(2):
                rows = slice(i * HD, (i + 1) * HD)
                ins = nc.scalar.copy(kz[rows, j:j + tiles, i, :],
                                     src[rows, 0:tiles * S].rearrange("p (c s) -> p c s", s=S))
            return ins

        def act_layer1(act, l):
            b = Book()
            act.dma_start(prow[:, 0:R1], a["prow1"][bass.ds(l, 1)].rearrange("o p n -> (o p) n")
                          .broadcast_to([P, R1])).then_inc(s["rows_in"], 16)
            zero = [0] * RAW
            act_split(act, b, l, PLAN1, zero, USES1, 2)
            act.wait_ge(s["cols_ready"], 1)
            act_turn(act, b, C_LN1)
            act_split(act, b, l, PLAN1, zero, USES1, AHEAD)
            act_norm(act, b, None)
            for g, (c0, w) in enumerate(groups(IN1)):
                n = len(by_columns("", D, c0, w))
                if g == CONV_AFTER + 1:
                    for f in range(2):
                        bank, k, _ = conv_fill(b)
                        act.wait_ge(tp_full[bank], k)
                        nc.scalar.copy(xT[:, 2 * f:2 * f + 2, :], tp[bank][:, :].rearrange("p (c s) -> p c s", s=S))\
                            .then_inc(s["conv_seen"], 1)
                    gate_fill(b)
                act_split(act, b, l, PLAN1, zero, USES1, b.unit + n + AHEAD)
                full = stream_done(b, (2 * (g % 2), 2 * (g % 2) + 1), n)
                if g == 0:
                    act.wait_ge(s["rstd_ready"], 1)
                for t in range(T):
                    wait(act, full[t])
                    nc.scalar.activation(z1[:, t, c0:c0 + w], acc[2 * (g % 2) + t][:, 0:w], ACT.Identity,
                                         scale=rstd[:, t:t + 1]).then_inc(s["z_act"], 1)
                if g == QK_GROUP:
                    act.wait_ge(s["z_act"], 2 * (g + 1))
                    nc.scalar.activation(sq1[:, :, :], z1[:, :, 0:QK1 * HD], ACT.Square).then_inc(s["sq_ready"], 1)
            act.wait_ge(s["z_act"], 2 * len(groups(IN1)))
            act.wait_ge(s["gate_abs"], 1)
            tick(act, b, act_chain, nc.scalar.activation(g_e[:, :], g_e[:, :], ACT.Exp))
            nc.scalar.activation(g_e[:, :], g_e[:, :], ACT.Ln, bias=1.0).then_inc(s["gate_ln"], 1)
            zxo = z1[:, :, ZXO:ZXO + LSTM * HD]
            nc.scalar.activation(zxo, zxo, ACT.Sigmoid).then_inc(s["xo_ready"], 1)
            for f in range(5):
                bank, k, _ = heads_fill(b)
                act.wait_ge(tp_full[bank], k)
                copy_heads(hT1, kz1, f, 3, tp[bank], 2).then_inc(s["heads_t"], 1)
            act.wait_ge(s["conv_done"], 1)
            nc.scalar.activation(hT1[:, 6:8, :], hT1[:, 6:8, :], ACT.Silu)
            for i in range(2):
                rows = slice(i * HD, (i + 1) * HD)
                ins = nc.scalar.activation(kz1[rows, 4:6, i, :], hT1[rows, 8:10, :], ACT.Silu)
            ins.then_inc(s["silu_conv"], 1)
            gcol_fill(b)
            act.wait_ge(s["gcol_ready"], 1)
            nc.scalar.activation(floor[:, :, :], gcol[:, :, 1, :], ACT.Exp).then_inc(s["floor_ready"], 1)
            act_heads(act, b, HEADS1)
            bank, n, _, k = y_fill(b)
            act.wait_ge(tp_full[bank], n)
            nc.scalar.activation(a_hi[:, 3:5, :], tp[bank][:, :].rearrange("p (c s) -> p c s", s=S), ACT.Copy)\
                .then_inc(s["pair_hi"], 1)
            act_split(act, b, l, PLAN1, zero, USES1, b.unit + DC + AHEAD)
            stream_done(b, range(4), DC)
            b.mark("x_new", 4)
            act_turn(act, b, C_LN2)
            act_norm(act, b, (s["x_new"], b.marks["x_new"]))
            act_split(act, b, l, PLAN1, zero, USES1, b.unit + RING)
            gs = groups(FF1)
            for g, (c0, w) in enumerate(gs):
                n = len(by_columns("", D, c0, w))
                act_split(act, b, l, PLAN1, zero, USES1, b.unit + n + AHEAD)
                full = stream_done(b, (2 * (g % 2), 2 * (g % 2) + 1), n)
                if g == 0:
                    act.wait_ge(s["rstd_ready"], 2)
                if g >= 2:
                    act.wait_ge(s["act_ready"], g - 1)
                for t in range(T):
                    wait(act, full[t])
                    ins = nc.scalar.activation(act_out[g % 2][:, t, :], acc[2 * (g % 2) + t][:, 0:w], ACT.Relu,
                                               scale=rstd[:, t:t + 1])
                ins.then_inc(s["relu_out"], 1)
                if g:
                    act_hidden(act, b, g - 1, gs[g - 1][1])
            act_hidden(act, b, len(gs) - 1, gs[-1][1])
            act_split(act, b, l, PLAN1, zero, USES1, len(PLAN1))
            layer_end(act, "act", b)

        def dve_layer1(dve, l):
            b = Book()
            nc.vector.tensor_copy(pcol[:, 0:C1], pcol1[:, bass.ds(l, 1), :].rearrange("p o n -> p (o n)"))\
                .then_inc(s["cols_ready"], 1)
            dve.wait_ge(s["cols_ready"], 1)
            dve_split(dve, b, PLAN1, 2)
            dve_turn(dve, b, C_LN1)
            dve_split(dve, b, PLAN1, AHEAD)
            dve_norm(dve, b)
            for g, (c0, w) in enumerate(groups(IN1)):
                n = len(by_columns("", D, c0, w))
                dve_split(dve, b, PLAN1, b.unit + min(2, n) + AHEAD)
                if g == 1:
                    dve.wait_ge(const_in, 16 * n_const)
                    dve.wait_ge(s["rows_in"], 16)
                    gain = prow[:, 0:4 * HD].rearrange("p (y d) -> p y d", d=HD)
                    for t in range(T):
                        nc.vector.tensor_tensor(rope_gc[:, t], rope_c[:, t], gain, ALU.mult)
                        for i in range(2):
                            to, frm = slice(i * 32, i * 32 + 32), slice(32 - i * 32, 64 - i * 32)
                            ins = nc.vector.tensor_tensor(rope_gs[:, t, :, to], rope_s[:, t, :, to], gain[:, :, frm],
                                                          ALU.mult)
                    ins.then_inc(s["tables_ready"], 1)
                if g == QK_GROUP + 1:
                    dve.wait_ge(s["z_act"], 2 * (QK_GROUP + 1))
                    dve.wait_ge(s["tables_ready"], 1)
                    for h0, nh, y in TYPES1:
                        for t in range(T):
                            ins = nc.vector.tensor_tensor(by_head(qk[:, :, :])[:, t, h0:h0 + nh, :],
                                                          by_head(z1[:, :, 0:QK1 * HD])[:, t, h0:h0 + nh, :],
                                                          rope_gc[:, t, y:y + 1, :].broadcast_to([P, nh, HD]), ALU.mult)
                    ins.then_inc(s["rope_a_ready"], 1)
                dve_split(dve, b, PLAN1, b.unit + n + AHEAD)
                if g == QK_GROUP + 1:
                    m = T * QK1
                    dve.wait_ge(s["sq_ready"], 1)
                    tick(dve, b, dve_chain, nc.vector.tensor_reduce(ssq[:, 0:m].rearrange("p (t h) -> p t h", t=T),
                                                                    by_head(sq1[:, :, :]), X, ALU.add))
                    nc.vector.tensor_scalar(msq[:, 0:m], ssq[:, 0:m], 1.0 / HD, EPS, ALU.mult, ALU.add)\
                        .then_inc(s["ms_ready"], 1)
                stream_done(b, (2 * (g % 2), 2 * (g % 2) + 1), n)
            conv_fill(b), conv_fill(b)
            bank, k, _ = gate_fill(b)
            dve.wait_ge(tp_full[bank], k)
            nc.vector.tensor_scalar(g_in[:, :], tp[bank][0:LSTM, 0:S], pcol[0:LSTM, C_IB:C_IB + 1], None, ALU.add)
            nc.vector.tensor_scalar(g_f[:, :], tp[bank][0:LSTM, S:2 * S], pcol[0:LSTM, C_FB:C_FB + 1], None,
                                    ALU.add).then_inc(s["gates_seen"], 1)
            dve.wait_ge(s["gates_seen"], 1)
            nc.vector.scalar_tensor_tensor(out=g_e[:, :], in0=g_f[:, :], scalar=-1.0, in1=g_f[:, :], op0=ALU.mult,
                                           op1=ALU.min).then_inc(s["gate_abs"], 1)
            dve.wait_ge(s["rope_a_ready"], 1)
            dve.wait_ge(s["rope_b_ready"], 1)
            tick(dve, b, dve_chain, nc.vector.tensor_tensor(qk[:, :, :], qk[:, :, :], qk_b[:, :, :], ALU.add))
            dve.wait_ge(s["rsh_ready"], 1)
            qh = qk[:, :, :].rearrange("p t (h d) -> p (t h) d", d=HD)
            nc.vector.tensor_tensor(qh, qh, rstd_h[:, 0:T * QK1].unsqueeze(2).broadcast_to([P, T * QK1, HD]),
                                    ALU.mult).then_inc(s["qk_ready"], 1)
            dve.wait_ge(s["conv_seen"], 2)
            for j in range(TAPS):
                for c in range(4):
                    wcol = pcol[:, C_CONV + c * TAPS + TAPS - 1 - j:C_CONV + c * TAPS + TAPS - j]
                    if j == 0:
                        ins = nc.vector.tensor_scalar(hT1[:, 6 + c, :], xT[:, c, :], wcol,
                                                      pcol[:, C_CONVB + c:C_CONVB + c + 1], ALU.mult, ALU.add)
                    else:
                        ins = nc.vector.scalar_tensor_tensor(out=hT1[:, 6 + c, j:S], in0=xT[:, c, 0:S - j],
                                                             scalar=wcol, in1=hT1[:, 6 + c, j:S], op0=ALU.mult,
                                                             op1=ALU.add)
                if j < TAPS - 1:
                    tick(dve, b, dve_chain, ins)
            ins.then_inc(s["conv_done"], 1)
            dve.wait_ge(s["gate_ln"], 1)
            tick(dve, b, dve_chain, nc.vector.scalar_tensor_tensor(out=g_f[:, :], in0=g_f[:, :], scalar=0.0,
                                                                   in1=g_e[:, :], op0=ALU.min, op1=ALU.subtract))
            tick(dve, b, dve_chain, nc.vector.tensor_tensor_scan(g_cum[:, :], ones[:, :], g_f[:, :], 0.0, ALU.mult,
                                                                 ALU.add))
            tick(dve, b, dve_chain, nc.vector.tensor_tensor(g_u[:, :], g_in[:, :], g_cum[:, :], ALU.subtract))
            tick(dve, b, dve_chain, nc.vector.tensor_tensor_scan(g_m[:, :], g_u[:, :], g_u[:, :], 0.0, ALU.max,
                                                                 ALU.max))
            nc.vector.tensor_scalar(g_row[:, 0, :], g_m[:, :], -1.0, None, ALU.mult)
            nc.vector.scalar_tensor_tensor(out=g_row[:, 1, :], in0=g_cum[:, :], scalar=-1.0, in1=g_m[:, :],
                                           op0=ALU.mult, op1=ALU.subtract).then_inc(s["gate_rows"], 1)
            for f in range(5):
                heads_fill(b)
            bank, k, _ = gcol_fill(b)
            dve.wait_ge(tp_full[bank], k)
            nc.vector.tensor_copy(gcol[:, :, :, :].rearrange("p t i h -> p (t i h)"), tp[bank][:, 0:4 * LSTM])\
                .then_inc(s["gcol_ready"], 1)
            dve_heads(dve, b, HEADS1)
            dve.wait_ge(s["prob_ready"], len(HEADS1))
            dve.wait_ge(s["floor_ready"], 1)
            tick(dve, b, dve_chain, nc.vector.scalar_tensor_tensor(out=dabs[:, :, :], in0=den[:, :, :], scalar=-1.0,
                                                                   in1=den[:, :, :], op0=ALU.mult, op1=ALU.max))
            tick(dve, b, dve_chain, nc.vector.tensor_tensor(dabs[:, :, :], dabs[:, :, :], floor[:, :, :], ALU.max))
            tick(dve, b, dve_chain, nc.vector.reciprocal(drec[:, :, :], dabs[:, :, :]))
            dve.wait_ge(s["units_used"], b.unit)
            dve.wait_ge(acc_full[2], b.marks["acc_full2"])
            m = T * LSTM
            nc.vector.tensor_tensor(lstm_h[:, :, :].rearrange("p t (h d) -> p (t h) d", d=HD),
                                    acc[2][:, :].rearrange("p (m d) -> p m d", d=HD),
                                    drec[:, :, :].rearrange("p t h -> p (t h)").unsqueeze(2).broadcast_to([P, m, HD]),
                                    ALU.mult).then_inc(s["lstm_seen"], 1)
            dve.wait_ge(s["lstm_seen"], 1)
            dve.wait_ge(s["xo_ready"], 1)
            tick(dve, b, dve_chain, nc.vector.tensor_tensor(lstm_h[:, :, :], lstm_h[:, :, :],
                                                            z1[:, :, ZXO:ZXO + LSTM * HD], ALU.mult))
            tick(dve, b, dve_chain, nc.vector.tensor_tensor(lstm_q[:, :, :], lstm_h[:, :, :], lstm_h[:, :, :], ALU.mult))
            tick(dve, b, dve_chain, nc.vector.tensor_reduce(ssq[:, 0:m].rearrange("p (t h) -> p t h", t=T),
                                                            by_head(lstm_q[:, :, :]), X, ALU.add))
            nc.vector.tensor_scalar(msq[:, 0:m], ssq[:, 0:m], 1.0 / HD, EPS, ALU.mult, ALU.add)\
                .then_inc(s["ms_ready"], 1)
            dve.wait_ge(s["rsh_ready"], 2)
            hh = lstm_h[:, :, :].rearrange("p t (h d) -> p (t h) d", d=HD)
            tick(dve, b, dve_chain, nc.vector.tensor_tensor(hh, hh, rstd_h[:, 0:m].unsqueeze(2)
                                                            .broadcast_to([P, m, HD]), ALU.mult))
            g = prow[:, R_MN:R_MN + LSTM * HD].unsqueeze(1).broadcast_to([P, T, LSTM * HD])
            nc.vector.tensor_tensor(lstm_h[:, :, :], lstm_h[:, :, :], g, ALU.mult).then_inc(s["y_ready"], 1)
            bank, n, _, k = y_fill(b)
            dve.wait_ge(s["pair_hi"], k)
            nc.vector.tensor_tensor(a_lo[:, 3:5, :], tp[bank][:, :].rearrange("p (c s) -> p c s", s=S),
                                    a_hi[:, 3:5, :].bitcast(F32), ALU.subtract).then_inc(s["pair_lo"], 1)
            dve_split(dve, b, PLAN1, b.unit + DC + AHEAD)
            dve_add_x(dve, b, 1.0, DC)
            dve_turn(dve, b, C_LN2)
            dve_norm(dve, b)
            dve_split(dve, b, PLAN1, b.unit + RING)
            gs = groups(FF1)
            for g, (c0, w) in enumerate(gs):
                n = len(by_columns("", D, c0, w))
                dve_split(dve, b, PLAN1, b.unit + n + AHEAD)
                stream_done(b, (2 * (g % 2), 2 * (g % 2) + 1), n)
                dve.wait_ge(s["relu_out"], g + 1)
                r = act_out[g % 2][:, :, :]
                nc.vector.tensor_tensor(r, r, r, ALU.mult).then_inc(s["act_ready"], 1)
                b.mark("act_ready")
                if g:
                    dve_hidden(dve, b, g - 1, gs[g - 1][1])
            dve_hidden(dve, b, len(gs) - 1, gs[-1][1])
            dve_split(dve, b, PLAN1, len(PLAN1))
            dve_add_x(dve, b, 1.0, FF1 // P)
            dve.wait_ge(s["x_new"], b.marks["x_new"])
            layer_end(dve, "dve", b)

        def pool_layer1(pool):
            b = Book()
            pool_norm(pool, b)
            pool.wait_ge(s["tables_ready"], 1)
            pool.wait_ge(s["z_act"], 2 * (QK_GROUP + 1))
            for h0, n, y in TYPES1:
                zz = by_head(z1[:, :, 0:QK1 * HD])[:, :, h0:h0 + n, :]
                for t in range(T):
                    for i in range(2):
                        to, frm = slice(i * 32, i * 32 + 32), slice(32 - i * 32, 64 - i * 32)
                        ins = nc.gpsimd.tensor_tensor(by_head(qk_b[:, :, :])[:, t, h0:h0 + n, to], zz[:, t, :, frm],
                                                      rope_gs[:, t, y:y + 1, to].broadcast_to([P, n, 32]), ALU.mult)
            ins.then_inc(s["rope_b_ready"], 1)
            pool.wait_ge(s["ms_ready"], 1)
            m = T * QK1
            nc.gpsimd.tensor_tensor(rstd_h[:, 0:m], msq[:, 0:m], half[:, 0:m], ALU.pow).then_inc(s["rsh_ready"], 1)
            pool.wait_ge(s["qk_ready"], 1)
            zero_halves(kz1)
            pool.wait_ge(s["ms_ready"], 2)
            m = T * LSTM
            nc.gpsimd.tensor_tensor(rstd_h[:, 0:m], msq[:, 0:m], half[:, 0:m], ALU.pow).then_inc(s["rsh_ready"], 1)
            pool_norm(pool, b)
            pool_end(pool)

        def pool_end(pool):
            pool.wait_ge(layer_done, 3)
            pool.sem_clear(range(min(nums), max(nums) + 1))
            for e in go.values():
                pool.sem_inc(e, 1)

        FG2 = groups(FF2)

        def pe_ffn2(pe, b, need):
            pe_turn(pe, b, lambda t, c: x[:, t, c * P:(c + 1) * P], need)
            hid0 = b.marks.get("hid", 0)
            for g, (c0, w) in enumerate(FG2):
                n = len(by_columns("", D, c0, w))
                k = b.mark("silu")
                pe_stream(pe, b, PLAN2, n, a_hi, a_lo, [0, 1], [(s["silu_done"], k)] * 2,
                          lambda i: (s["turn_lo"], b.turns) if g == 0 and i == 0 else None)
                if g:
                    pe_hidden(pe, b, g - 1, FG2[g - 1][1])
                pe_stream(pe, b, PLAN2, n, a_hi, a_lo, [2, 3], [(s["act_ready"], k)] * 2)
            pe_hidden(pe, b, len(FG2) - 1, FG2[-1][1])
            pe_stream(pe, b, PLAN2, FF2 // P, h_hi, h_lo, range(4), released_x(b),
                      lambda n: (s["hid_lo"], hid0 + n // 2 + 1) if n % 2 == 0 else None)
            b.mark("x_new", 4)

        def act_ffn2(act, b, l, base, need):
            gain = b.mark("ffn") - 1
            act_turn(act, b, 2 * DC * gain)
            act_norm(act, b, need)
            act_split(act, b, l, PLAN2, base, USES2, b.unit + RING)
            rn = b.marks["norm"]
            for g, (c0, w) in enumerate(FG2):
                n = len(by_columns("", D, c0, w))
                act_split(act, b, l, PLAN2, base, USES2, b.unit + n + AHEAD)
                full = stream_done(b, (0, 1), n)
                if g == 0:
                    act.wait_ge(s["rstd_ready"], rn)
                k = b.mark("silu")
                if k > 1:
                    act.wait_ge(s["act_ready"], k - 1)
                for t in range(T):
                    wait(act, full[t])
                    ins = nc.scalar.activation(silu_out[:, t, 0:w], acc[t][:, 0:w], ACT.Silu, scale=rstd[:, t:t + 1])
                ins.then_inc(s["silu_done"], 1)
                if g:
                    act_hidden(act, b, g - 1, FG2[g - 1][1])
                act_split(act, b, l, PLAN2, base, USES2, b.unit + n + AHEAD)
                stream_done(b, (2, 3), n)
            act_hidden(act, b, len(FG2) - 1, FG2[-1][1])
            act_split(act, b, l, PLAN2, base, USES2, b.unit + FF2 // P + AHEAD)
            stream_done(b, range(4), FF2 // P)
            b.mark("x_new", 4)

        def dve_ffn2(dve, b):
            gain = b.mark("ffn") - 1
            dve_turn(dve, b, 2 * DC * gain)
            dve_norm(dve, b)
            dve_split(dve, b, PLAN2, b.unit + RING)
            rn = b.marks["norm"]
            for g, (c0, w) in enumerate(FG2):
                n = len(by_columns("", D, c0, w))
                dve_split(dve, b, PLAN2, b.unit + n + AHEAD)
                stream_done(b, (0, 1), n)
                if g:
                    dve_hidden(dve, b, g - 1, FG2[g - 1][1])
                dve_split(dve, b, PLAN2, b.unit + n + AHEAD)
                full = stream_done(b, (2, 3), n)
                dve.wait_ge(s["silu_done"], b.mark("silu"))
                if g == 0:
                    dve.wait_ge(s["rstd_ready"], rn)
                for t in range(T):
                    wait(dve, full[t])
                    ins = nc.vector.scalar_tensor_tensor(out=act_out[g % 2][:, t, 0:w], in0=acc[2 + t][:, 0:w],
                                                         scalar=rstd[:, t:t + 1], in1=silu_out[:, t, 0:w],
                                                         op0=ALU.mult, op1=ALU.mult)
                ins.then_inc(s["act_ready"], 1)
            dve_hidden(dve, b, len(FG2) - 1, FG2[-1][1])
            dve_split(dve, b, PLAN2, b.unit + FF2 // P + AHEAD)
            dve_add_x(dve, b, 0.5, FF2 // P)

        NG2 = len(IN2_GROUPS)
        PLAIN2 = len(groups(ZG))
        Z_DVE2 = PLAIN2 + 2 * (NG2 - PLAIN2)

        def z2_released(g):
            if g < PLAIN2:
                return [(s["z_act"], g + 1), (s["z_dve"], g + 1)]
            k = PLAIN2 + 2 * (g - PLAIN2)
            return [(s["z_dve"], k + 1), (s["z_dve"], k + 2)]

        def x_need(b):
            k = b.marks["x_new"]
            return lambda f: (s["x_new"], k - 2 + 2 * (f // 2))

        TILES2 = [c + i * P for c in (ZQA, ZQS, ZKA) for i in range(4)] + [ZKS]
        HEADS_AFTER = PLAIN2 + 2

        def pe_layer2(pe):
            b = Book()
            pe_ffn2(pe, b, lambda f: None)
            pe_turn(pe, b, lambda t, c: x[:, t, c * P:(c + 1) * P], x_need(b))
            for g, (c0, w) in enumerate(IN2_GROUPS):
                pe_stream(pe, b, PLAN2, len(by_columns("", D, c0, w)), a_hi, a_lo, [2 * (g % 2), 2 * (g % 2) + 1],
                          z2_released(g), lambda i: (s["turn_lo"], b.turns) if g == 0 and i == 0 else None)
                if g != HEADS_AFTER:
                    continue
                pe.wait_ge(s["normed"], 1)
                for f in range(7):
                    bank, n, before = heads_fill(b)
                    wait(pe, before)
                    for i, c in enumerate(TILES2[2 * f:2 * f + 2]):
                        for t in range(T):
                            mm = nc.tensor.transpose(tp[bank][:, i * S + t * P:i * S + (t + 1) * P],
                                                     z2[:, t, c:c + P], ident[:, :])
                    mm.then_inc(tp_full[bank], 1)
            pe_heads(pe, b, HEADS2)
            for n in range(2):
                pe_stream(pe, b, PLAN2, 2, a_hi, a_lo, [0, 1], [(s["na_out"], n + 1)] * 2,
                          lambda i: (s["pair_lo"], 8) if n == 0 and i == 0 else None)
                pe_stream(pe, b, PLAN2, 2, a_hi, a_lo, [2, 3], [(s["sw_out"], n + 1)] * 2, None, NAW // P)
            pe_turn(pe, b, lambda t, c: work[:, t * D + c * P:t * D + (c + 1) * P],
                    lambda f: (s["merged"], f // 2 + 1))
            pe_stream(pe, b, PLAN2, DC, a_hi, a_lo, range(4), released_x(b),
                      lambda n: (s["turn_lo"], b.turns) if n == 0 else None)
            b.mark("x_new", 4)
            pe_ffn2(pe, b, x_need(b))
            pe.wait_ge(s["units_used"], b.unit)
            layer_end(pe, "pe", b)

        def act_layer2(act, l):
            b = Book()
            base = [DEPTH * u for u in USES1]
            act.dma_start(prow[:, 0:R2], a["prow2"][bass.ds(l, 1)].rearrange("o p n -> (o p) n")
                          .broadcast_to([P, R2])).then_inc(s["rows_in"], 16)
            act_split(act, b, l, PLAN2, base, USES2, 2)
            act.wait_ge(s["cols_ready"], 1)
            act_ffn2(act, b, l, base, None)
            act.wait_ge(s["x_new"], b.marks["x_new"])
            act.dma_start(na_bias[:, :, :, :], na_skew[bass.ds(l, 1)].rearrange("o p t h k -> (o p) t h k"))\
                .then_inc(s["bias_in"], 16)
            act_turn(act, b, DC)
            act_norm(act, b, (s["x_new"], b.marks["x_new"]))
            rn = b.marks["norm"]
            for g, (c0, w) in enumerate(IN2_GROUPS):
                n = len(by_columns("", D, c0, w))
                if g == HEADS_AFTER + 1:
                    for f in range(7):
                        bank, k, _ = heads_fill(b)
                        m = len(TILES2[2 * f:2 * f + 2])
                        act.wait_ge(tp_full[bank], k)
                        copy_heads(hT2, kz2, f, 4, tp[bank], m).then_inc(s["heads_t"], 1)
                act_split(act, b, l, PLAN2, base, USES2, b.unit + n + AHEAD)
                full = stream_done(b, (2 * (g % 2), 2 * (g % 2) + 1), n)
                if g == 0:
                    act.wait_ge(s["rstd_ready"], rn)
                if g < PLAIN2:
                    wait(act, full[0])
                    nc.scalar.activation(z2[:, 0, c0:c0 + w], acc[2 * (g % 2)][:, 0:w], ACT.Identity,
                                         scale=rstd[:, 0:1]).then_inc(s["z_act"], 1)
                if g == PLAIN2 - 1:
                    act.wait_ge(s["z_act"], PLAIN2)
                    act.wait_ge(s["z_dve"], PLAIN2)
                    for h0, c1, m in RUNS2:
                        ins = nc.scalar.activation(sq2[:, :, h0 * HD:(h0 + m) * HD], z2[:, :, c1:c1 + m * HD],
                                                   ACT.Square)
                    ins.then_inc(s["sq_ready"], 1)
            act.wait_ge(s["z_dve"], Z_DVE2)
            zg = z2[:, :, ZG:ZG + 2 * D]
            nc.scalar.activation(zg, zg, ACT.Sigmoid).then_inc(s["g_ready"], 1)
            act_heads(act, b, HEADS2)
            act_split(act, b, l, PLAN2, base, USES2, b.unit + 8 + AHEAD)
            for n in range(2):
                stream_done(b, (0, 1), 2)
                stream_done(b, (2, 3), 2)
            act_turn(act, b, None)
            act_split(act, b, l, PLAN2, base, USES2, b.unit + DC + AHEAD)
            stream_done(b, range(4), DC)
            b.mark("x_new", 4)
            act_ffn2(act, b, l, base, (s["x_new"], b.marks["x_new"]))
            layer_end(act, "act", b)

        def dve_layer2(dve, l):
            b = Book()
            nc.vector.tensor_copy(pcol[:, 0:C2], pcol2[:, bass.ds(l, 1), :].rearrange("p o n -> p (o n)"))\
                .then_inc(s["cols_ready"], 1)
            dve.wait_ge(s["cols_ready"], 1)
            dve_split(dve, b, PLAN2, 2)
            dve_ffn2(dve, b)
            dve_turn(dve, b, DC)
            dve_norm(dve, b)
            rn = b.marks["norm"]
            nh = 2 * NA + SW + SW_KV
            for g, (c0, w) in enumerate(IN2_GROUPS):
                n = len(by_columns("", D, c0, w))
                dve_split(dve, b, PLAN2, b.unit + n + AHEAD)
                full = stream_done(b, (2 * (g % 2), 2 * (g % 2) + 1), n)
                if g == 0:
                    dve.wait_ge(s["rstd_ready"], rn)
                if g == PLAIN2:
                    dve.wait_ge(s["rows_in"], 16)
                for t in range(T):
                    k = acc[2 * (g % 2) + t][:, 0:w]
                    if g < PLAIN2 and t == 1:
                        wait(dve, full[t])
                        nc.vector.tensor_scalar(z2[:, t, c0:c0 + w], k, rstd[:, t:t + 1], None, ALU.mult)\
                            .then_inc(s["z_dve"], 1)
                    elif g >= PLAIN2:
                        wait(dve, full[t])
                        bg = prow[:, R2_BG + c0 - ZG:R2_BG + c0 - ZG + w]
                        nc.vector.scalar_tensor_tensor(out=z2[:, t, c0:c0 + w], in0=k, scalar=rstd[:, t:t + 1], in1=bg,
                                                       op0=ALU.mult, op1=ALU.add).then_inc(s["z_dve"], 1)
                if g == PLAIN2:
                    for y in range(4):
                        ins = nc.vector.tensor_scalar(gain2[:, y, :], prow[:, R2_GAIN + y * HD:R2_GAIN + (y + 1) * HD],
                                                      HD ** -0.5 if y % 2 == 0 else 1.0, None, ALU.mult)
                    dve.wait_ge(s["sq_ready"], 1)
                    tick(dve, b, dve_chain, nc.vector.tensor_reduce(ssq[:, 0:T * nh].rearrange("p (t h) -> p t h", t=T),
                                                                    by_head(sq2[:, :, :]), X, ALU.add))
                    nc.vector.tensor_scalar(msq[:, 0:T * nh], ssq[:, 0:T * nh], 1.0 / HD, EPS, ALU.mult, ALU.add)\
                        .then_inc(s["ms_ready"], 1)
                if g == PLAIN2 + 1:
                    dve.wait_ge(s["rsh_ready"], 1)
                    for h0, c1, m in RUNS2:
                        zz = by_head(z2[:, :, c1:c1 + m * HD])
                        r = rstd_h[:, 0:T * nh].rearrange("p (t h) -> p t h", t=T)[:, :, h0:h0 + m]
                        ins = nc.vector.tensor_tensor(zz, zz, r.unsqueeze(3).broadcast_to([P, T, m, HD]), ALU.mult)
                    tick(dve, b, dve_chain, ins)
                    for y, (c1, m) in enumerate(TYPES2):
                        for t in range(T):
                            zz = by_head(z2[:, :, c1:c1 + m * HD])[:, t]
                            ins = nc.vector.tensor_tensor(zz, zz, gain2[:, y:y + 1, :].broadcast_to([P, m, HD]),
                                                          ALU.mult)
                    ins.then_inc(s["normed"], 1)
            for f in range(7):
                heads_fill(b)
            dve.wait_ge(t5_in, 16)
            dve.wait_ge(s["bias_ready"], 1)
            dve_heads(dve, b, HEADS2)
            dve.wait_ge(s["g_ready"], 1)
            for n in range(2):
                for i, done in ((0, "na_out"), (2, "sw_out")):
                    dve_split(dve, b, PLAN2, b.unit + 2 + AHEAD)
                    full = stream_done(b, (i, i + 1), 2)
                    for t in range(T):
                        wait(dve, full[t])
                        c = ZG + (i // 2) * D + n * GROUP
                        to = work[:, t * D + n * GROUP:t * D + (n + 1) * GROUP] if i == 0 else act_out[0][:, t, :]
                        ins = nc.vector.tensor_tensor(to, acc[i + t][:, :], z2[:, t, c:c + GROUP], ALU.mult)
                    ins.then_inc(s[done], 1)
                dve.wait_ge(s["sw_out"], n + 1)
                both = work[:, :].rearrange("p (t d) -> p t d", t=T)[:, :, n * GROUP:(n + 1) * GROUP]
                nc.vector.tensor_tensor(both, both, act_out[0][:, :, :], ALU.add).then_inc(s["merged"], 1)
                dve.wait_ge(s["merged"], n + 1)
            dve_turn(dve, b, None)
            dve_split(dve, b, PLAN2, b.unit + DC + AHEAD)
            dve_add_x(dve, b, 1.0, DC)
            dve_ffn2(dve, b)
            dve.wait_ge(s["x_new"], b.marks["x_new"])
            layer_end(dve, "dve", b)

        def pool_layer2(pool):
            b = Book()
            pool_norm(pool, b)
            pool_norm(pool, b)
            pool.wait_ge(s["bias_in"], 16)
            nb = na_bias[:, :, :, :].rearrange("p t h k -> p (t h) k")
            nc.gpsimd.tensor_tensor(nb, nb, mask_n[:, :].unsqueeze(1).broadcast_to([P, T * NA, S]), ALU.add)\
                .then_inc(s["bias_ready"], 1)
            pool.wait_ge(s["ms_ready"], 1)
            nc.gpsimd.tensor_tensor(rstd_h[:, 0:T * 26], msq[:, 0:T * 26], half[:, 0:T * 26], ALU.pow)\
                .then_inc(s["rsh_ready"], 1)
            pool.wait_ge(s["rsh_ready"], 1)
            zero_halves(kz2)
            pool_norm(pool, b)
            pool_end(pool)

        @blk.tensor
        def _(pe):
            base_const(pe)
            with pe.Fori(0, DEPTH):
                pe_layer1(pe)
            nc.tensor.matmul(acc[0][0:SW, :], t5_tab[:, :], onehot[:, :], start=True, stop=True).then_inc(t5_read, 1)
            pe.wait_ge(t5_row, 1)
            with pe.Fori(0, DEPTH):
                pe_layer2(pe)

        @blk.scalar
        def _(act):
            base_const(act)
            with act.Fori(0, DEPTH) as l:
                act_layer1(act, l)
            act.wait_ge(skewed, 16 * DEPTH * GRID_H * GRID_H)
            with act.Fori(0, DEPTH) as l:
                act_layer2(act, l)

        @blk.vector
        def _(dve):
            base_const(dve)
            with dve.Fori(0, DEPTH) as l:
                dve_layer1(dve, l)
            dve.wait_ge(t5_read, 1)
            nc.vector.tensor_copy(t5_rel[:, :], acc[0][0:SW, :]).then_inc(t5_row, 1)
            with dve.Fori(0, DEPTH) as l:
                dve_layer2(dve, l)
            dve.sem_inc(x_final, 1)

        @blk.gpsimd
        def _(pool):
            base_const(pool)
            with pool.Fori(0, DEPTH):
                pool_layer1(pool)
            pool.wait_ge(t5_row, 1)
            pool.dma_start(t5_dram, t5_rel[:, :]).then_inc(t5_out, 16)
            pool.wait_ge(t5_out, 16)
            for t in range(T):
                src = bass.AP(t5_dram.tensor, S - 1 - t * P, [[REL, SW], [-1, P], [1, S]])
                pool.dma_start(t5_skew[:, t, :, :].rearrange("p h k -> h p k"), src).then_inc(t5_turned, 16)
            pool.wait_ge(t5_turned, 16 * T)
            pool.dma_start(t5_bias[:, :, :, :], t5_skew).then_inc(t5_in, 16)
            with pool.Fori(0, DEPTH):
                pool_layer2(pool)


def constants():
    f = np.float32
    c = {"ident": np.eye(P, dtype=f), "neg_half": np.full((P, 64), -0.5, f), "ones": np.ones((LSTM, S), f)}
    inv = f(10000.0) ** (-np.arange(0, HD, 2, dtype=f) / f(HD))
    ang = np.arange(S, dtype=f)[:, None] * inv[None, :]
    cos, sin = np.cos(ang), np.sin(ang)
    scale = np.array([HD ** -0.5, 1, HD ** -0.5, 1], f)

    def by_tile(v):
        return np.ascontiguousarray(v.reshape(T, P, *v.shape[1:]).swapaxes(0, 1))

    c["rope_c"] = by_tile(np.concatenate([cos, cos], -1)[:, None] * scale[:, None])
    c["rope_s"] = by_tile(np.concatenate([-sin, sin], -1)[:, None] * scale[:, None])
    q, k = np.arange(P)[:, None], np.arange(P)[None, :]
    own = np.where(k <= q, 0, NEG).astype(f)
    c["mask_m"] = np.concatenate([own, np.zeros((P, P), f), own], 1)
    c["mask_s"] = np.concatenate([own, np.where(q + P - k < WINDOW1, 0, NEG).astype(f), own], 1)
    c["pick"] = np.repeat(np.eye(LSTM, dtype=f)[:, :, None], P, 2)
    qc, kc = np.arange(P)[:, None] % GRID_W, np.arange(S)[None, :] % GRID_W
    first = np.clip(qc - NA_COLS // 2, 0, GRID_W - NA_COLS)
    c["mask_n"] = np.where((kc >= first) & (kc < first + NA_COLS), 0, NEG).astype(f)
    rel = np.arange(REL) - (S - 1)
    nb = BUCKETS // 2
    exact = nb // 2
    n = np.abs(rel)
    large = exact + (np.log(np.maximum(n, 1) / exact) / np.log(MAX_DIST / exact) * (nb - exact)).astype(np.int32)
    bucket = (rel > 0) * nb + np.where(n < exact, n, np.minimum(large, nb - 1))
    outside = np.where(n <= WINDOW2, 0, NEG)
    c["onehot"] = np.concatenate([np.arange(BUCKETS)[:, None] == bucket[None, :], outside[None]]).astype(f)
    return c


def reordered(w, axis, first, order):
    idx = np.arange(w.shape[axis])
    idx[first:first + len(order) * HD] = (first + np.array(order)[:, None] * HD + np.arange(HD)).ravel()
    return np.take(w, idx, axis)


def slabs(plan, weights):
    outs = np.zeros((DEPTH, len(plan) // 2, P, 2, HALF), np.float32)
    for u, (name, chunks, c0, w) in enumerate(plan):
        k0 = chunks[0]
        part = weights[name][:, k0 * P:(k0 + len(chunks)) * P, c0:c0 + w]
        part = part.reshape(DEPTH, len(chunks), P, w).transpose(0, 2, 1, 3)
        outs[:, u // 2, :, u % 2, :len(chunks) * w] = part.reshape(DEPTH, P, len(chunks) * w)
    return outs.reshape(-1, P, SLAB)


def columns(*parts):
    return np.concatenate([v.reshape(DEPTH, -1, P).transpose(2, 0, 1) for v in parts], 2)


def kernel(**inputs):
    from concourse import bacc
    from concourse.bass_utils import run_bass_kernel_spmd

    i = {k: np.ascontiguousarray(v) for k, v in inputs.items()}
    first = {n: sum(w for _, w in PARTS1[:k]) for k, (n, _) in enumerate(PARTS1)}
    i["w_in"] = reordered(i["w_in"], 2, first["sq"], SWA_ORDER)
    i["w_in"] = np.concatenate([i["w_in"][:, :, first[n]:first[n] + WIDTH1[n]] for n in ORDER1], 2)
    i["w_out"] = reordered(i["w_out"], 1, MOBA * HD + LSTM * HD, SWA_ORDER)
    i["w_in_2"] = reordered(i["w_in_2"], 2, ZQS, SW_ORDER)
    i["w_branch_sw_2"] = reordered(i["w_branch_sw_2"], 1, 0, SW_ORDER)
    f = np.float32
    gates = np.zeros((P, DEPTH, 2), f)
    gates[:LSTM, :, 0], gates[:LSTM, :, 1] = i["igate_b"].T, i["fgate_b"].T
    taps = i["conv_w"].reshape(DEPTH, TAPS, 4, P).transpose(3, 0, 2, 1).reshape(P, DEPTH, 4 * TAPS)
    arrays = {
        "x": i["x"],
        "slabs1": slabs(PLAN1, i), "slabs2": slabs(PLAN2, i),
        "pcol1": np.concatenate([columns(i["ln1"], i["ln2"]), taps, columns(i["conv_b"]), gates], 2),
        "pcol2": columns(i["ffn1_norm_2"], i["mix_norm_2"], i["ffn2_norm_2"]),
        "prow1": np.concatenate([i[k].reshape(DEPTH, 1, -1) for k in (
            "moba_q_norm", "moba_k_norm", "swa_q_norm", "swa_k_norm", "mlstm_norm", "swa_sinks")], 2),
        "prow2": np.concatenate([i[k].reshape(DEPTH, 1, -1) for k in (
            "b_gate_2", "na_q_norm_2", "na_k_norm_2", "sw_q_norm_2", "sw_k_norm_2", "sw_sink_2")], 2),
        "rpb": i["na_rpb_2"], "t5_rel_table_2": i["t5_rel_table_2"], **constants(),
    }
    nc = bacc.Bacc("TRN2", target_bir_lowering=False, num_devices=1)
    aps = {k: nc.dram_tensor(f"in_{k}", v.shape, mybir.dt.from_np(v.dtype), kind="ExternalInput").ap()
           for k, v in arrays.items()}
    out = nc.dram_tensor("out_x", (1, S, D), F32, kind="ExternalOutput").ap()
    build(nc, aps, out)
    r = run_bass_kernel_spmd(nc, [{f"in_{k}": np.ascontiguousarray(v) for k, v in arrays.items()}], core_ids=[0])
    return r.results[0]["out_x"]
```

```python
from contextlib import ExitStack

import numpy as np

import concourse.bass as bass
from concourse import mybir
from concourse.alu_op_type import AluOpType as ALU

F32 = mybir.dt.float32
F32R = mybir.dt.float32r
ACT = mybir.ActivationFunctionType
X = mybir.AxisListType.X

P = 128
S = 256
T = S // P
D = 1024
DC = D // P
DEPTH = 2
HD = 64
EPS = 1e-6
MASK = 1e30
HIGHEST = 3.0e38

FF1 = 4 * D
MOBA, LSTM, SWA, SWA_KV = 6, 4, 6, 2
WINDOW1 = 128
TAPS = 4
IN1 = 3 * MOBA * HD + (SWA + 2 * SWA_KV) * HD + 4 * LSTM * HD + 2 * LSTM
PARTS1 = (("mq", MOBA * HD), ("mk", MOBA * HD), ("mv", MOBA * HD), ("sq", SWA * HD), ("sk", SWA_KV * HD),
          ("sv", SWA_KV * HD), ("xqk", 2 * LSTM * HD), ("xv", LSTM * HD), ("xo", LSTM * HD), ("xi", LSTM), ("xf", LSTM))
ORDER1 = ("mq", "sq", "mk", "sk", "xqk", "xi", "xf", "mv", "sv", "xv", "xo")
WIDTH1 = dict(PARTS1)
ZXQK, ZXI, ZXF, ZMV, ZSV, ZXV, ZXO = (sum(WIDTH1[m] for m in ORDER1[:ORDER1.index(n)])
                                      for n in ("xqk", "xi", "xf", "mv", "sv", "xv", "xo"))
QK1 = 2 * MOBA + SWA + SWA_KV
GRID_W = 64
GRID_H = S // GRID_W
NA, SW, SW_KV = 8, 8, 2
NA_ROWS, NA_COLS = 8, 16
RPB_H, RPB_W = 2 * NA_ROWS - 1, 2 * NA_COLS - 1
WINDOW2 = 128
BUCKETS, MAX_DIST = 32, 128
FF2 = 2816
NAW, SWQW, SWKVW = NA * HD, SW * HD, SW_KV * HD
IN2 = 3 * NAW + SWQW + 2 * SWKVW + 2 * D
ZQA, ZKA, ZVA = 0, NAW, 2 * NAW
ZQS = 3 * NAW
ZKS = ZQS + SWQW
ZVS = ZKS + SWKVW
ZG = ZVS + SWKVW
REL = 2 * S

SWA_ORDER = [h + k * (SWA // SWA_KV) for h in range(SWA // SWA_KV) for k in range(SWA_KV)]
SW_ORDER = [h + k * (SW // SW_KV) for h in range(SW // SW_KV) for k in range(SW_KV)]

HALF = 1024
SLAB = 2 * HALF
RAW, RING = 3, 4
PROBS = 4
TAIL = 3
AHEAD = 3
GROUP = 512

C_LN1, C_LN2, C_CONV, C_CONVB, C_IB, C_FB, C1 = 0, 8, 16, 32, 36, 37, 38
R_GAIN, R_MN, R_SINK, R1 = 0, 256, 512, 518
C2 = 3 * DC
R2_BG, R2_GAIN, R2_SINK, R2 = 0, 2048, 2304, 2312


def groups(width):
    return [(c, min(GROUP, width - c)) for c in range(0, width, GROUP)]


def by_columns(name, rows, c0, w):
    chunks = rows // P
    n = HALF // w
    while chunks % n or (chunks // n) % 2 and chunks // n > 1:
        n -= 1
    return [(name, list(range(k, k + n)), c0, w) for k in range(0, chunks, n)]


def by_rows(name, order):
    return [(name, [k], 0, D) for k in order]


IN2_GROUPS = groups(ZG) + [(ZG + c, w) for c, w in groups(2 * D)]
Y_AT = 4
OUT_ORDER = [0, 1, 2, 5, 6, 7, 3, 4]


def plan1():
    plan = []
    for c0, w in groups(IN1):
        plan += by_columns("w_in", D, c0, w)
    plan += by_rows("w_out", OUT_ORDER)
    for c0, w in groups(FF1):
        plan += by_columns("w_up", D, c0, w)
    return plan + by_rows("w_down", range(FF1 // P))


def plan2():
    plan = []

    def ffn(n):
        for c0, w in groups(FF2):
            plan.extend(by_columns(f"ffn{n}_w_gate_2", D, c0, w))
            plan.extend(by_columns(f"ffn{n}_w_up_2", D, c0, w))
        plan.extend(by_rows(f"ffn{n}_w_down_2", range(FF2 // P)))

    ffn(1)
    for c0, w in IN2_GROUPS:
        plan.extend(by_columns("w_in_2", D, c0, w))
    for c0, w in groups(D):
        plan.extend(by_columns("w_branch_na_2", NAW, c0, w))
        plan.extend(by_columns("w_branch_sw_2", SWQW, c0, w))
    plan.extend(by_rows("w_out_2", range(DC)))
    ffn(2)
    return plan


PLAN1, PLAN2 = plan1(), plan2()
SLABS1, SLABS2 = len(PLAN1) // 2, len(PLAN2) // 2
USES1 = [len(range(s, SLABS1, RAW)) for s in range(RAW)]
USES2 = [len(range(s, SLABS2, RAW)) for s in range(RAW)]


class Book:

    def __init__(self):
        self.unit = 0
        self.made = 0
        self.fills = {}
        self.release = {}
        self.turns = 0
        self.marks = {}

    def fill(self, bank, released_by=None):
        n = self.fills[bank] = self.fills.get(bank, 0) + 1
        before = self.release.get(bank)
        self.release[bank] = released_by
        return n, before

    def mark(self, name, n=1):
        self.marks[name] = self.marks.get(name, 0) + n
        return self.marks[name]


def build(nc, a, out):
    ctx = ExitStack()
    with ctx:
        at = [-(-nc.sbuf_base // 64) * 64]

        def sb(name, shape, dt=F32, offset=None):
            size = 4 * int(np.prod(shape[1:]))
            if offset is None:
                offset = at[0]
                at[0] += -(-size // 32) * 32
            return nc.alloc_sbuf_tensor_at(name, shape, dt, offset=offset)

        def sem(name):
            return ctx.enter_context(nc.semaphore(name))

        x = sb("x_res", [P, T, D])
        work = sb("work", [P, 2048])
        a_hi = sb("a_hi", [P, DC, S], F32R)
        a_lo = sb("a_lo", [P, DC, S], F32R)
        raw = [sb(f"raw{i}", [P, SLAB]) for i in range(RAW)]
        w_hi = [sb(f"w_hi{i}", [P, HALF], F32R) for i in range(RING)]
        w_lo = [sb(f"w_lo{i}", [P, HALF], F32R) for i in range(RING)]
        hidden0 = at[0]
        h_hi = sb("h_hi", [P, FF1 // P, S], F32R)
        h_lo = sb("h_lo", [P, FF1 // P, S], F32R)
        act0 = at[0]
        act_out = [sb(f"act_out{i}", [P, T, GROUP]) for i in range(2)]
        silu0 = at[0]
        silu_out = sb("silu_out", [P, T, GROUP])
        ident = sb("ident", [P, P])
        mask_n = sb("mask_n", [P, S])
        onehot = sb("onehot", [BUCKETS + 1, REL])
        t5_tab = sb("t5_tab", [BUCKETS + 1, SW])
        t5_bias0 = at[0]
        t5_bias = sb("t5_bias", [P, T, SW, S])
        pcol1 = sb("pcol1", [P, DEPTH, C1])
        pcol2 = sb("pcol2", [P, DEPTH, C2])
        pcol = sb("pcol", [P, C1])
        prow = sb("prow", [P, R2])
        half = sb("neg_half", [P, 64])
        ssq = sb("ssq", [P, 64])
        msq = sb("msq", [P, 64])
        rstd_h = sb("rstd_h", [P, 64])
        ss2 = sb("ss2", [P, T])
        ms2 = sb("ms2", [P, T])
        rstd = sb("rstd", [P, T])
        nsink = sb("neg_sink", [P, 8])
        nmx = sb("nmx", [P, PROBS, T])
        esum = sb("esum", [P, PROBS, T])
        esink = sb("esink", [P, PROBS, T])
        tot = sb("tot", [P, PROBS, T])
        rinv = sb("rinv", [P, PROBS, T])
        gcol = sb("gcol", [P, T, 2, LSTM])
        floor = sb("floor", [P, T, LSTM])
        den = sb("den", [P, T, LSTM])
        dabs = sb("dabs", [P, T, LSTM])
        drec = sb("drec", [P, T, LSTM])
        assert at[0] <= nc.sbuf_usable_end, (at[0], nc.sbuf_usable_end)

        o = [hidden0]

        def over(name, shape):
            t = sb(name, shape, offset=o[0])
            o[0] += 4 * int(np.prod(shape[1:]))
            return t

        z1 = over("z1", [P, T, IN1])
        qk = over("qk", [P, T, QK1 * HD])
        kz1 = over("keys_t1", [P, 6, 2, S])
        hT1 = over("heads_t1", [P, 10, S])
        xT = over("conv_in", [P, 4, S])
        gates = [over(f"gate{i}", [LSTM, S]) for i in range(3)]
        assert o[0] <= hidden0 + 8 * FF1 // P * S
        o[0] = hidden0
        z2 = over("z2", [P, T, IN2])
        na_bias = over("na_bias", [P, T, NA, S])
        hT2 = over("heads_t2", [P, 8, S])
        probT2 = over("prob_t2", [P, 2 * GROUP])
        assert o[0] <= hidden0 + 8 * FF1 // P * S
        sq2_at = hidden0 + 4 * (T * IN2 + T * NA * S)
        sq2 = sb("sq2", [P, T, 26 * HD], offset=sq2_at)
        gain2 = sb("gain2", [P, 4, HD], offset=sq2_at + 4 * T * 26 * HD)
        assert sq2_at + 4 * (T * 26 * HD + 4 * HD) <= hidden0 + 8 * FF1 // P * S
        kz2 = sb("keys_t2", [P, 5, 2, S], offset=act0)
        qk_b = sb("qk_b", [P, T, QK1 * HD], offset=hidden0 + 4 * T * (IN1 + QK1 * HD))
        sq1 = sb("sq1", [P, T, QK1 * HD], offset=hidden0 + 4 * (T * (IN1 + QK1 * HD) + 12 * S))
        o[0] = t5_bias0
        rope_c = over("rope_c", [P, T, 4, HD])
        rope_s = over("rope_s", [P, T, 4, HD])
        mask_m = over("mask_m", [P, 3 * P])
        mask_s = over("mask_s", [P, 3 * P])
        pick = over("pick", [LSTM, LSTM, P])
        ones = over("ones", [LSTM, S])
        g_row = over("g_row", [LSTM, 2, S])
        g_u = over("g_u", [LSTM, S])
        assert o[0] <= t5_bias0 + 4 * T * SW * S
        g_in, g_f, g_e = gates
        g_cum, g_m = g_e, g_f
        conv_sig = sb("conv_sig", [P, 4, S], offset=hidden0 + 4 * T * (IN1 + LSTM * HD))
        lstm_h = sb("lstm_h", [P, T, LSTM * HD], offset=hidden0 + 4 * T * IN1)
        lstm_q = sb("lstm_q", [P, T, LSTM * HD], offset=hidden0 + 4 * T * (IN1 + QK1 * HD))
        t5_rel = sb("t5_rel", [SW, REL], offset=silu0)

        prob = [work[:, i * GROUP:(i + 1) * GROUP] for i in range(PROBS)]
        probT1 = silu_out[:, :, :].rearrange("p t n -> p (t n)")
        rope_gc = act_out[0][:, :, :].rearrange("p t (y d) -> p t y d", d=HD)[:, :, 0:4, :]
        rope_gs = act_out[1][:, :, :].rearrange("p t (y d) -> p t y d", d=HD)[:, :, 0:4, :]

        acc = [ctx.enter_context(nc.psum_tensor(f"acc{i}", [P, GROUP], F32)) for i in range(4)]
        sc = [ctx.enter_context(nc.psum_tensor(f"sc{i}", [P, GROUP], F32)) for i in range(2)]
        tp = [ctx.enter_context(nc.psum_tensor(f"tp{i}", [P, GROUP], F32)) for i in range(2)]

        const_in = sem("const_in")
        x_in = sem("x_in")
        t5_dram = nc.dram_tensor("t5_by_distance", [SW, REL], F32).ap()
        na_skew = nc.dram_tensor("na_skew", [DEPTH, P, T, NA, S], F32).ap()
        skewed = sem("na_skewed")
        slab_in = [sem(f"slab_in{i}") for i in range(RAW)]
        slab_free = sem("slab_free")
        streamed = sem("layer_streamed")
        t5_read = sem("t5_read")
        t5_row = sem("t5_row")
        t5_out = sem("t5_out")
        t5_turned = sem("t5_turned")
        t5_skew = nc.dram_tensor("t5_skew", [P, T, SW, S], F32).ap()
        t5_in = sem("t5_in")
        base_in = sem("base_in")
        x_final = sem("x_final")
        stored = sem("stored")
        go = {e: sem(f"go_{e}") for e in ("act", "dve", "pe")}

        layer_done = sem("layer_done")
        names = """act_chain dve_chain pool_chain unit_hi unit_lo units_used
            tp_full0 tp_full1 acc_full0 acc_full1 acc_full2 acc_full3 sc_full0 sc_full1
            cols_ready rows_in ssx_ready msx_ready rstd_ready turn_hi turn_lo x_new
            z_act z_dve relu_out act_ready hid_hi hid_lo silu_done
            sq_ready ms_ready rsh_ready tables_ready normed rope_a_ready rope_b_ready rope_sum qk_ready conv_seen gates_seen
            gate_abs gate_ln gate_rows gcol_ready floor_ready conv_done silu_conv xo_ready heads_t
            kz_ready sink_ready sig_conv score_seen d_seen exp_done prob_ready probT_ready pair_hi pair_lo
            lstm_seen y_ready bias_in bias_ready g_ready na_out sw_out merged""".split()
        s = {n: sem(n) for n in names}
        nums = [v.num for v in [layer_done, *s.values()]]
        assert sorted(nums) == list(range(min(nums), min(nums) + len(nums)))
        tp_full = [s["tp_full0"], s["tp_full1"]]
        acc_full = [s[f"acc_full{i}"] for i in range(4)]
        sc_full = [s["sc_full0"], s["sc_full1"]]
        act_chain, dve_chain, pool_chain = s["act_chain"], s["dve_chain"], s["pool_chain"]

        def wait(eng, what):
            if what is not None:
                eng.wait_ge(what[0], what[1])

        def tick(eng, b, chain, ins):
            ins.then_inc(chain, 1)
            eng.wait_ge(chain, b.mark("chain"))


        def act_split(act, b, l, plan, slabs1, uses, to):
            while b.made < min(to, len(plan)):
                u = b.made
                name, chunks, c0, w = plan[u]
                n = len(chunks) * w
                j, slot = u // 2, (u // 2) % RAW
                if u % 2 == 0:
                    base = slabs1[slot]
                    act.wait_ge(slab_in[slot], (l * uses[slot] + base + j // RAW + 1) * 16)
                if u >= RING:
                    act.wait_ge(s["units_used"], u - RING + 1)
                nc.scalar.activation(w_hi[u % RING][:, 0:n], raw[slot][:, (u % 2) * HALF:(u % 2) * HALF + n],
                                     ACT.Copy).then_inc(s["unit_hi"], 1)
                b.made += 1

        def dve_split(dve, b, plan, to):
            while b.made < min(to, len(plan)):
                u = b.made
                name, chunks, c0, w = plan[u]
                n = len(chunks) * w
                slot = (u // 2) % RAW
                dve.wait_ge(s["unit_hi"], u + 1)
                nc.vector.tensor_tensor(w_lo[u % RING][:, 0:n], raw[slot][:, (u % 2) * HALF:(u % 2) * HALF + n],
                                        w_hi[u % RING][:, 0:n].bitcast(F32), ALU.subtract).then_inc(s["unit_lo"], 1)
                b.made += 1
                if u % 2:
                    dve.wait_ge(s["unit_lo"], u + 1)
                    dve.sem_inc(slab_free, 1)

        def products(b, plan, u, hi, lo, banks, first, last, shift, only=None):
            name, chunks, c0, w = plan[u]
            cols = min(w, GROUP)
            for i, c in enumerate(chunks):
                for t in range(T):
                    for n in range(w // cols):
                        bank = n * T + t
                        if only is not None and bank != only:
                            continue
                        o_ = banks[bank][:, 0:cols]
                        col = slice(i * w + n * cols, i * w + (n + 1) * cols)
                        xh, xl = hi[:, c + shift, t * P:(t + 1) * P], lo[:, c + shift, t * P:(t + 1) * P]
                        wh, wl = w_hi[u % RING][:, col], w_lo[u % RING][:, col]
                        nc.tensor.matmul(o_, xh, wh, start=first and i == 0, stop=False)
                        nc.tensor.matmul(o_, xh, wl, start=False, stop=False)
                        mm = nc.tensor.matmul(o_, xl, wh, start=False, stop=last and i == len(chunks) - 1)
                        if last and i == len(chunks) - 1 and bank != len(banks) - 1:
                            mm.then_inc(acc_full[acc.index(banks[bank])], 1)
            return mm

        def pe_stream(pe, b, plan, n_units, hi, lo, banks, released_by, need=None, shift=0, late=None):
            for k, i in enumerate(banks):
                _, before = b.fill(("acc", i), released_by[k])
                wait(pe, before)
            to = [acc[i] for i in banks]
            tail = min(TAIL if len(banks) == 4 else 1, n_units)
            for n in range(n_units):
                if need is not None:
                    wait(pe, need(n))
                pe.wait_ge(s["unit_lo"], b.unit + n + 1)
                if n < n_units - tail:
                    products(b, plan, b.unit + n, hi, lo, to, n == 0, False, shift).then_inc(s["units_used"], 1)
            if tail == 1:
                products(b, plan, b.unit + n, hi, lo, to, n == 0, True, shift).then_inc(s["units_used"], 1)
            else:
                for bank in range(len(banks)):
                    if bank == len(banks) - 1 and late is not None:
                        late()
                    for n in range(n_units - tail, n_units):
                        mm = products(b, plan, b.unit + n, hi, lo, to, n == 0, n == n_units - 1, shift, bank)
                        if bank == len(banks) - 1:
                            mm.then_inc(s["units_used"], 1)
            b.unit += n_units
            for i in banks[:-1]:
                b.mark(f"acc_full{i}")

        def pe_steps(pe, b, plan, n_units, hi, lo, banks, released_by, need):
            before = [b.fill(("acc", i), r)[1] for i, r in zip(banks, released_by)]
            units = list(range(n_units))
            first = b.unit
            b.unit += n_units
            for i in banks[:-1]:
                b.mark(f"acc_full{i}")

            def step():
                n = units.pop(0)
                if n == 0:
                    for w in before:
                        wait(pe, w)
                wait(pe, need(n))
                pe.wait_ge(s["unit_lo"], first + n + 1)
                products(b, plan, first + n, hi, lo, [acc[i] for i in banks], n == 0, n == n_units - 1, 0)\
                    .then_inc(s["units_used"], 1)

            return step

        def stream_done(b, banks, n_units):
            b.unit += n_units
            return [(acc_full[i], b.mark(f"acc_full{i}")) for i in banks[:-1]] + [(s["units_used"], b.unit)]

        def turn_fills(b):
            for f in range(DC // 2):
                b.turns += 1
                q = b.mark("tp") - 1
                bank = q % 2
                n, before = b.fill(("tp", bank), (s["turn_lo"], b.turns))
                yield f, bank, n, before, b.turns

        def pe_turn(pe, b, src, need):
            fills = list(turn_fills(b))

            def do(n):
                for f, bank, _, before, k in fills[:n]:
                    wait(pe, need(f))
                    wait(pe, before)
                    for i in range(2):
                        for t in range(T):
                            c = 2 * f + i
                            mm = nc.tensor.transpose(tp[bank][:, i * S + t * P:i * S + (t + 1) * P],
                                                     src(t, c), ident[:, :])
                    mm.then_inc(tp_full[bank], 1)
                del fills[:n]

            return do

        def turned(b, turn, per=2, last=None):
            last = b.turns if last is None else last

            def need(n):
                if n in (3 - per, 4 - per):
                    turn(1)
                return (s["turn_lo"], last - 3 + n * per // 2)

            return need

        def act_turn(act, b, gain):
            fills = list(turn_fills(b))

            def do(n):
                for f, bank, k, _, _ in fills[:n]:
                    act.wait_ge(tp_full[bank], k)
                    for i in range(2):
                        c = 2 * f + i
                        g = 1.0 if gain is None else pcol[:, gain + c:gain + c + 1]
                        ins = nc.scalar.activation(a_hi[:, c, :], tp[bank][:, i * S:(i + 1) * S], ACT.Identity,
                                                   scale=g)
                    ins.then_inc(s["turn_hi"], 1)
                del fills[:n]

            return do

        def dve_turn(dve, b, gain):
            fills = list(turn_fills(b))

            def do(n):
                for f, bank, _, _, k in fills[:n]:
                    dve.wait_ge(s["turn_hi"], k)
                    for i in range(2):
                        c = 2 * f + i
                        g = 1.0 if gain is None else pcol[:, gain + c:gain + c + 1]
                        ins = nc.vector.scalar_tensor_tensor(out=a_lo[:, c, :], in0=tp[bank][:, i * S:(i + 1) * S],
                                                             scalar=g, in1=a_hi[:, c, :].bitcast(F32),
                                                             op0=ALU.mult, op1=ALU.subtract)
                    ins.then_inc(s["turn_lo"], 1)
                del fills[:n]

            return do

        def act_next(b, split, turn, more=0):
            split(b.unit + 1)
            turn(2)
            split(b.unit + more + 2)
            turn(1)
            split(b.unit + more + 3)
            turn(1)

        def dve_next(b, split, add, turn):
            split(b.unit + 1)
            if add is not None:
                add(3)
            turn(1)
            if add is not None:
                add(1)
            turn(1)
            split(b.unit + 2)
            turn(1)
            split(b.unit + 3)
            turn(1)

        def act_norm(act, b, need):
            wait(act, need)
            for t in range(T):
                ins = nc.scalar.activation(work[:, t * D:(t + 1) * D], x[:, t, :], ACT.Square,
                                           accum_out=ss2[:, t:t + 1])
            ins.then_inc(s["ssx_ready"], 1)
            b.mark("norm")

        def dve_norm(dve, b):
            n = b.mark("norm")
            dve.wait_ge(s["ssx_ready"], n)
            nc.vector.tensor_scalar(ms2[:, :], ss2[:, :], 1.0 / D, EPS, ALU.mult, ALU.add).then_inc(s["msx_ready"], 1)

        def zero_halves(kz):
            nc.gpsimd.memset(kz[HD:P, :, 0, :], 0.0)
            nc.gpsimd.memset(kz[0:HD, :, 1, :], 0.0).then_inc(s["kz_ready"], 1)

        def pool_norm(pool, b):
            n = b.mark("norm")
            pool.wait_ge(s["msx_ready"], n)
            nc.gpsimd.tensor_tensor(rstd[:, :], ms2[:, :], half[:, 0:T], ALU.pow).then_inc(s["rstd_ready"], 1)

        def dve_add_x(dve, b, scale, n_units):
            banks = list(enumerate(stream_done(b, range(4), n_units)))

            def do(k):
                for i, full in banks[:k]:
                    wait(dve, full)
                    n, t = i // T, i % T
                    xs = x[:, t, n * GROUP:(n + 1) * GROUP]
                    nc.vector.scalar_tensor_tensor(out=xs, in0=acc[i][:, :], scalar=scale, in1=xs, op0=ALU.mult,
                                                   op1=ALU.add).then_inc(s["x_new"], 1)
                    b.mark("x_new")
                del banks[:k]

            return do

        def released_x(b):
            m = b.marks.get("x_new", 0)
            return [(s["x_new"], m + 1 + i) for i in range(4)]

        def layer_end(eng, name, b):
            eng.sem_inc(layer_done, 1)
            eng.wait_ge(go[name], 1)
            eng.sem_clear(go[name])

        blk = ctx.enter_context(nc.Block())
        BASE = (("pcol1", pcol1), ("ident", ident), ("neg_half", half))
        CONSTS = ((pcol2, "pcol2"), (rope_c, "rope_c"), (rope_s, "rope_s"), (mask_m, "mask_m"), (mask_s, "mask_s"),
                  (pick, "pick"), (mask_n, "mask_n"), (ones, "ones"), (onehot, "onehot"))
        n_const = len(CONSTS) + 2
        STAGES = 4

        @blk.sync
        def _(sp):
            x_tiles = a["x"].rearrange("o (t p) d -> p (o t) d", p=P)
            for name, dst in BASE:
                sp.dma_start(dst[:], a[name]).then_inc(base_in, 16)
            for t in range(T):
                sp.dma_start(x[:, t, :], x_tiles[:, t, :]).then_inc(x_in, 16)
            for k in range(RAW):
                sp.dma_start(raw[k][:, :], a["slabs1"][k]).then_inc(slab_in[k], 16)
            for dst, name in CONSTS:
                sp.dma_start(dst[:], a[name]).then_inc(const_in, 16)
            sp.dma_start(t5_tab[0:BUCKETS, :], a["t5_rel_table_2"]).then_inc(const_in, 16)
            sp.dma_start(t5_tab[BUCKETS:BUCKETS + 1, :], a["ones"][0:1, 0:SW]).then_inc(const_in, 16)
            rounds = DEPTH * SLABS1 // RAW
            for stage in range(STAGES):
                with sp.Fori(1 + (rounds - 1) * stage // STAGES, 1 + (rounds - 1) * (stage + 1) // STAGES) as i:
                    for k in range(RAW):
                        src = a["slabs1"][bass.ds(i * RAW + k, 1)].rearrange("o p n -> (o p) n")
                        sp.wait_ge(slab_free, i * RAW + (k + 1 - RAW))
                        sp.dma_start(raw[k][:, :], src).then_inc(slab_in[k], 16)
                for lr in range(stage * DEPTH * GRID_H // STAGES, (stage + 1) * DEPTH * GRID_H // STAGES):
                    l, r = lr // GRID_H, lr % GRID_H
                    t, i = r // 2, r % 2
                    for kr in range(GRID_H):
                        row = (NA_ROWS - 1 - r + kr) * RPB_W + NA_COLS - 1
                        src = bass.AP(a["rpb"].tensor, l * (NA * RPB_H * RPB_W) + row,
                                      [[RPB_H * RPB_W, NA], [-1, GRID_W], [1, GRID_W]])
                        dst = na_skew[l, i * GRID_W:(i + 1) * GRID_W, t, :, kr * GRID_W:(kr + 1) * GRID_W]
                        sp.dma_start(dst.rearrange("p h k -> h p k"), src).then_inc(skewed, 16)
            done = DEPTH * SLABS1
            whole = SLABS2 // RAW
            with sp.Fori(0, DEPTH) as l:
                with sp.Fori(0, whole) as i:
                    for k in range(RAW):
                        src = a["slabs2"][bass.ds(l * SLABS2 + i * RAW + k, 1)].rearrange("o p n -> (o p) n")
                        sp.wait_ge(slab_free, l * SLABS2 + i * RAW + (done + k + 1 - RAW))
                        sp.dma_start(raw[k][:, :], src).then_inc(slab_in[k], 16)
                for k in range(SLABS2 - RAW * whole):
                    src = a["slabs2"][bass.ds(l * SLABS2 + (RAW * whole + k), 1)].rearrange("o p n -> (o p) n")
                    sp.wait_ge(slab_free, l * SLABS2 + (done + RAW * whole + k + 1 - RAW))
                    sp.dma_start(raw[k][:, :], src).then_inc(slab_in[k], 16)
                sp.wait_ge(slab_free, l * SLABS2 + (done + SLABS2))
                sp.sem_inc(streamed, 1)
            sp.wait_ge(x_final, 1)
            sp.dma_start(out.rearrange("o (t p) d -> p (o t) d", p=P), x[:, :, :]).then_inc(stored, 16)
            sp.wait_ge(stored, 16)

        def x_need(b, to_come=0):
            k = b.marks.get("x_new", 0) + to_come
            return lambda f: (s["x_new"], k - 2 + 2 * (f // 2))

        def x_chunk(t, c):
            return x[:, t, c * P:(c + 1) * P]

        GCOL_AT = 7
        QK_GROUP = (QK1 * HD - 1) // GROUP
        CONV_AFTER = (ZXF + LSTM - 1) // GROUP + 1

        def pe_layer1(pe):
            b = Book()
            turn = pe_turn(pe, b, x_chunk, lambda f: None)
            turn(2)
            for g, (c0, w) in enumerate(groups(IN1)):
                pe_stream(pe, b, PLAN1, len(by_columns("", D, c0, w)), a_hi, a_lo,
                          [2 * (g % 2), 2 * (g % 2) + 1], [(s["z_act"], 2 * g + 1), (s["z_act"], 2 * g + 2)],
                          turned(b, turn) if g == 0 else None)
                if g != CONV_AFTER:
                    continue
                pe.wait_ge(s["z_act"], 2 * CONV_AFTER)
                for f in range(2):
                    bank, n, before = conv_fill(b)
                    wait(pe, before)
                    for i in range(2):
                        for t in range(T):
                            c = ZXQK + (2 * f + i) * P
                            mm = nc.tensor.transpose(tp[bank][:, i * S + t * P:i * S + (t + 1) * P],
                                                     z1[:, t, c:c + P], ident[:, :])
                    mm.then_inc(tp_full[bank], 1)
                bank, n, before = gate_fill(b)
                wait(pe, before)
                for i, c in enumerate((ZXI, ZXF)):
                    for t in range(T):
                        mm = nc.tensor.transpose(tp[bank][0:LSTM, i * S + t * P:i * S + (t + 1) * P],
                                                 z1[:, t, c:c + LSTM], ident[:, :])
                mm.then_inc(tp_full[bank], 1)
            pe.wait_ge(s["qk_ready"], 1)
            fills = [(f, *heads_fill(b)) for f in FILLS1]
            gcol_bank, _, gcol_before = gcol_fill(b)

            def turn_heads(n):
                for f, bank, _, before in fills[:n]:
                    wait(pe, before)
                    for i in range(2):
                        for t in range(T):
                            c = (2 * f + i) * P
                            mm = nc.tensor.transpose(tp[bank][:, i * S + t * P:i * S + (t + 1) * P],
                                                     qk[:, t, c:c + P], ident[:, :])
                    mm.then_inc(tp_full[bank], 1)
                del fills[:n]

            def beside(i):
                if i != GCOL_AT:
                    return
                wait(pe, gcol_before)
                pe.wait_ge(s["gate_rows"], 1)
                for t in range(T):
                    for j in range(2):
                        c = (2 * t + j) * LSTM
                        mm = nc.tensor.transpose(acc[gcol_bank][:, c:c + LSTM], g_row[:, j, t * P:(t + 1) * P],
                                                 ident[0:LSTM, 0:LSTM])
                mm.then_inc(acc_full[gcol_bank], 1)

            turn_heads(2)
            pe_heads(pe, b, HEADS1, lambda: turn_heads(3), beside)
            bank, _, before, k = y_fill(b)

            def chunk_ready(n):
                if n == Y_AT:
                    pe.wait_ge(s["y_ready"], 1)
                    wait(pe, before)
                    for i in range(2):
                        for t in range(T):
                            mm = nc.tensor.transpose(tp[bank][:, i * S + t * P:i * S + (t + 1) * P],
                                                     lstm_h[:, t, i * P:(i + 1) * P], ident[:, :])
                    mm.then_inc(tp_full[bank], 1)
                return (s["pair_lo"], min(n, OUT_ORDER.index(3)) + 1)

            b_x = released_x(b)
            turn = pe_turn(pe, b, x_chunk, x_need(b, 4))
            pe_stream(pe, b, PLAN1, DC, a_hi, a_lo, range(4), b_x, chunk_ready, late=lambda: turn(1))
            turn(1)
            b.mark("x_new", 4)
            gs = groups(FF1)
            for g, (c0, w) in enumerate(gs):
                pe_stream(pe, b, PLAN1, len(by_columns("", D, c0, w)), a_hi, a_lo,
                          [2 * (g % 2), 2 * (g % 2) + 1], [(s["relu_out"], g + 1)] * 2,
                          turned(b, turn) if g == 0 else None)
                if g:
                    pe_hidden(pe, b, g - 1, gs[g - 1][1])
            pe_hidden(pe, b, len(gs) - 1, gs[-1][1])
            pe_stream(pe, b, PLAN1, FF1 // P, h_hi, h_lo, range(4), released_x(b),
                      lambda n: (s["hid_lo"], n // 2 + 1) if n % 2 == 0 else None)
            b.mark("x_new", 4)
            pe.wait_ge(s["units_used"], b.unit)
            layer_end(pe, "pe", b)

        def hidden_fills(b, width):
            for f in range(width // (2 * P)):
                k = b.mark("hid")
                q = b.mark("tp") - 1
                bank = q % 2
                n, before = b.fill(("tp", bank), (s["hid_lo"], k))
                yield f, bank, n, before, k

        def pe_hidden(pe, b, g, width):
            pe.wait_ge(s["act_ready"], b.mark("act_ready"))
            for f, bank, n, before, k in hidden_fills(b, width):
                wait(pe, before)
                for i in range(2):
                    for t in range(T):
                        c = (2 * f + i) * P
                        mm = nc.tensor.transpose(tp[bank][:, i * S + t * P:i * S + (t + 1) * P],
                                                 act_out[g % 2][:, t, c:c + P], ident[:, :])
                mm.then_inc(tp_full[bank], 1)

        def act_hidden(act, b, g, width):
            for f, bank, n, before, k in hidden_fills(b, width):
                act.wait_ge(tp_full[bank], n)
                c = g * (GROUP // P) + 2 * f
                nc.scalar.activation(h_hi[:, c:c + 2, :], tp[bank][:, :].rearrange("p (c s) -> p c s", s=S),
                                     ACT.Copy).then_inc(s["hid_hi"], 1)

        def dve_hidden(dve, b, g, width):
            for f, bank, n, before, k in hidden_fills(b, width):
                dve.wait_ge(s["hid_hi"], k)
                c = g * (GROUP // P) + 2 * f
                nc.vector.tensor_tensor(h_lo[:, c:c + 2, :], tp[bank][:, :].rearrange("p (c s) -> p c s", s=S),
                                        h_hi[:, c:c + 2, :].bitcast(F32), ALU.subtract).then_inc(s["hid_lo"], 1)

        def next_tp(b, released_by):
            q = b.mark("tp") - 1
            bank = q % 2
            n, before = b.fill(("tp", bank), released_by)
            return bank, n, before

        def conv_fill(b):
            return next_tp(b, (s["conv_seen"], b.mark("conv")))

        def gate_fill(b):
            return next_tp(b, (s["gates_seen"], 1))

        def heads_fill(b):
            return next_tp(b, (s["heads_t"], b.mark("heads")))

        def gcol_fill(b):
            _, before = b.fill(("acc", 0), (s["gcol_ready"], 1))
            return 0, b.mark("acc_full0"), before

        def y_fill(b):
            k = b.mark("pair")
            return (*next_tp(b, (s["pair_lo"], k)), k)

        HEADS1 = []
        for h in range(MOBA):
            HEADS1.append(dict(kind="soft", q=h // 2, k=h // 2, half=h % 2, v=ZMV + h * HD, sink=None,
                               chunk=h // 2, mask=mask_m))
        for i, h in enumerate(SWA_ORDER):
            HEADS1.append(dict(kind="soft", q=3 + i // 2, k=3, half=i % 2, v=ZSV + (i % 2) * HD, sink=h,
                               chunk=5 + i // 2, mask=mask_s))
        for h in range(LSTM):
            HEADS1.append(dict(kind="lstm", q=6 + h // 2, k=4 + h // 2, half=h % 2, v=ZXV + h * HD, h=h))
        HEADS2 = []
        for h in range(NA):
            HEADS2.append(dict(kind="full", q=h // 2, k=h // 2, half=h % 2, v=ZVA + h * HD, sink=None,
                               chunk=h // 2, bias=na_bias, h=h))
        for i, h in enumerate(SW_ORDER):
            HEADS2.append(dict(kind="full", q=4 + i // 2, k=4, half=i % 2, v=ZVS + (i % 2) * HD, sink=h,
                               chunk=4 + i // 2, bias=t5_bias, h=h))

        def head_fills(b, heads):
            soft = [i for i, h in enumerate(heads) if h["kind"] != "lstm"]
            plan = []
            for i, h in enumerate(heads):
                e = {}
                rel = (s["prob_ready" if h["kind"] == "lstm" else "score_seen"], i + 1)
                e["sc"] = (i % 2, *b.fill(("sc", i % 2), rel))
                e["tp"] = next_tp(b, (s["probT_ready"], i + 1))
                if h["kind"] == "lstm":
                    m = h["h"]
                    _, before = b.fill(("acc", m % 2), (s["d_seen"], m + 1))
                    e["d"] = (m % 2, b.mark(f"acc_full{m % 2}"), before)
                    if m == 0:
                        _, before = b.fill(("acc", 2), (s["lstm_seen"], 1))
                        e["o"] = (2, b.mark("acc_full2"), before)
                    else:
                        e["o"] = plan[-1]["o"]
                elif i % 2 == 0:
                    pair = b.mark("pair")
                    bank = 2 + (pair - 1) % 2
                    _, before = b.fill(("acc", bank), (s["pair_lo"], pair))
                    e["o"] = (bank, b.mark(f"acc_full{bank}"), before)
                    e["pair"] = pair
                else:
                    e["o"] = plan[-1]["o"]
                    e["pair"] = plan[-1]["pair"]
                plan.append(e)
            return plan

        def pe_heads(pe, b, heads, after_two=None, beside=None):
            fills = head_fills(b, heads)
            hT, kz, probT = (hT1, kz1, probT1) if heads is HEADS1 else (hT2, kz2, probT2)
            z = z1 if heads is HEADS1 else z2
            full = heads is HEADS2
            n = len(heads)

            def scores(i):
                h = heads[i]
                bank, k, before = fills[i]["sc"]
                q, kk = hT[:, h["q"], :], kz[:, h["k"], h["half"], :]
                pe.wait_ge(s["heads_t"], 7 if full else 2 if i < 4 else 4 if i < MOBA else 5)
                if i == 0:
                    pe.wait_ge(s["kz_ready"], 1)
                if h["kind"] == "lstm":
                    if h["h"] == 0:
                        pe.wait_ge(s["silu_conv"], 3)
                    dbank, dk, dbefore = fills[i]["d"]
                    wait(pe, dbefore)
                    nc.tensor.matmul(acc[dbank][:, 0:P], pick[:, h["h"], :], g_u[:, 0:P], start=True, stop=True)
                    nc.tensor.matmul(acc[dbank][:, P:3 * P], pick[:, h["h"], :], g_u[:, :], start=True,
                                     stop=True).then_inc(acc_full[dbank], 1)
                wait(pe, before)
                if full:
                    nc.tensor.matmul(sc[bank][:, 0:S], q[:, 0:P], kk, start=True, stop=True)
                    nc.tensor.matmul(sc[bank][:, S:2 * S], q[:, P:S], kk, start=True, stop=True)\
                        .then_inc(sc_full[bank], 1)
                else:
                    nc.tensor.matmul(sc[bank][:, 0:P], q[:, 0:P], kk[:, 0:P], start=True, stop=True)
                    nc.tensor.matmul(sc[bank][:, P:3 * P], q[:, P:S], kk, start=True, stop=True)\
                        .then_inc(sc_full[bank], 1)

            def turn(i):
                bank, k, before = fills[i]["tp"]
                pe.wait_ge(s["prob_ready"], i + 1)
                wait(pe, before)
                blocks = 4 if full else 3
                src = prob[i % PROBS]
                for j in range(blocks):
                    frm = (j % 2) * 2 + j // 2 if full else j
                    mm = nc.tensor.transpose(tp[bank][:, j * P:(j + 1) * P], src[:, frm * P:(frm + 1) * P],
                                             ident[:, :])
                mm.then_inc(tp_full[bank], 1)

            def values(i):
                h = heads[i]
                bank, k, before = fills[i]["o"]
                pT = probT[:, (i % 2) * GROUP:(i % 2 + 1) * GROUP]
                pe.wait_ge(s["probT_ready"], i + 1)
                if i == 0 and not full:
                    pe.wait_ge(s["z_act"], 2 * len(groups(IN1)))
                v = [z[:, t, h["v"]:h["v"] + HD] for t in range(T)]
                if h["kind"] == "lstm":
                    m = h["h"]
                    if m == 0:
                        wait(pe, before)
                    ob = acc[bank][:, :].rearrange("p (t h d) -> p t h d", t=T, d=HD)
                    nc.tensor.matmul(ob[:, 0, m, :], pT[:, 0:P], v[0], start=True, stop=True)
                    nc.tensor.matmul(ob[:, 1, m, :], pT[:, P:2 * P], v[0], start=True, stop=False)
                    mm = nc.tensor.matmul(ob[:, 1, m, :], pT[:, 2 * P:3 * P], v[1], start=False, stop=True)
                    if m == LSTM - 1:
                        mm.then_inc(acc_full[bank], 1)
                    return
                if h["half"] == 0:
                    wait(pe, before)
                p0 = h["half"] * HD
                ob = acc[bank][p0:p0 + HD, 0:S]
                if full:
                    nc.tensor.matmul(ob, v[0], pT[:, 0:S], start=True, stop=False)
                    mm = nc.tensor.matmul(ob, v[1], pT[:, S:2 * S], start=False, stop=True)
                else:
                    nc.tensor.matmul(ob, v[0], pT[:, 0:S], start=True, stop=False)
                    mm = nc.tensor.matmul(ob[:, P:S], v[1], pT[:, 2 * P:3 * P], start=False, stop=True)
                if h["half"] == 1:
                    mm.then_inc(acc_full[bank], 1)

            for i in range(PROBS):
                scores(i)
                if i == 1 and after_two is not None:
                    after_two()
            for i in range(n + 1):
                if i < n:
                    turn(i)
                if i + PROBS < n:
                    scores(i + PROBS)
                if i >= 1:
                    values(i - 1)
                if beside is not None:
                    beside(i)

        def dve_heads(dve, b, heads, beside=None):
            fills = head_fills(b, heads)
            full = heads is HEADS2
            n = len(heads)
            tiles = [slice(0, S), slice(S, 2 * S)] if full else [slice(0, P), slice(P, 3 * P)]

            dve.wait_ge(s["sink_ready"], 1)

            def first(i):
                h, p = heads[i], i % PROBS
                bank, k, before = fills[i]["sc"]
                if i >= PROBS:
                    tb, tk, _ = fills[i - PROBS]["tp"]
                    dve.wait_ge(tp_full[tb], tk)
                if h["kind"] == "lstm":
                    dbank, dk, _ = fills[i]["d"]
                    dve.wait_ge(acc_full[dbank], dk)
                    nc.vector.tensor_tensor(prob[p][:, 0:3 * P], acc[dbank][:, 0:3 * P], mask_m[:, :],
                                            ALU.add).then_inc(s["d_seen"], 1)
                    return
                dve.wait_ge(sc_full[bank], k)
                for t in range(T):
                    extra = h["bias"][:, t, h["h"], :] if full else h["mask"][:, tiles[t]]
                    start = HIGHEST if h["sink"] is None else nsink[:, h["sink"]:h["sink"] + 1]
                    ins = nc.vector.tensor_tensor_reduce(prob[p][:, tiles[t]], sc[bank][:, tiles[t]], extra, 1.0,
                                                         start, ALU.add, ALU.min, nmx[:, p, t:t + 1])
                ins.then_inc(s["score_seen"], 1)

            def second(i):
                h, p = heads[i], i % PROBS
                dve.wait_ge(s["exp_done"], i + 1)
                if h["kind"] == "lstm":
                    bank, k, before = fills[i]["sc"]
                    dve.wait_ge(sc_full[bank], k)
                    for t in range(T):
                        ins = nc.vector.scalar_tensor_tensor(out=prob[p][:, tiles[t]], in0=sc[bank][:, tiles[t]],
                                                             scalar=HD ** -0.5, in1=prob[p][:, tiles[t]],
                                                             op0=ALU.mult, op1=ALU.mult,
                                                             accum_out=den[:, t, h["h"]:h["h"] + 1])
                    ins.then_inc(s["prob_ready"], 1)
                    return
                total = esum
                if h["sink"] is not None:
                    tick(dve, b, dve_chain, nc.vector.tensor_tensor(tot[:, p, :], esum[:, p, :], esink[:, p, :],
                                                                    ALU.add))
                    total = tot
                tick(dve, b, dve_chain, nc.vector.reciprocal(rinv[:, p, :], total[:, p, :]))
                for t in range(T):
                    ins = nc.vector.tensor_scalar(prob[p][:, tiles[t]], prob[p][:, tiles[t]], rinv[:, p, t:t + 1],
                                                  None, ALU.mult)
                ins.then_inc(s["prob_ready"], 1)

            def pair(i):
                h = heads[i]
                if h["kind"] == "lstm" or h["half"] == 0:
                    return
                bank = fills[i]["o"][0]
                k = fills[i]["pair"]
                dve.wait_ge(s["pair_hi"], k)
                nc.vector.tensor_tensor(a_lo[:, h["chunk"], :], acc[bank][:, 0:S],
                                        a_hi[:, h["chunk"], :].bitcast(F32), ALU.subtract).then_inc(s["pair_lo"], 1)

            for i in range(n + 5):
                if 2 <= i < n + 2:
                    second(i - 2)
                if i < n:
                    first(i)
                if beside is not None:
                    beside(i)
                if i >= 5:
                    pair(i - 5)

        def sinks(heads):
            r = R_SINK if heads is HEADS1 else R2_SINK
            return prow[:, r:r + 8]

        def act_heads(act, b, heads, beside=None):
            fills = head_fills(b, heads)
            full = heads is HEADS2
            n = len(heads)
            tiles = [slice(0, S), slice(S, 2 * S)] if full else [slice(0, P), slice(P, 3 * P)]
            used = 2 * S if full else 3 * P
            probT = probT2 if full else probT1

            def exps(i):
                h, p = heads[i], i % PROBS
                if h["kind"] == "lstm":
                    act.wait_ge(s["d_seen"], h["h"] + 1)
                    for t in range(T):
                        m = gcol[:, t, 0, h["h"]:h["h"] + 1]
                        ins = nc.scalar.activation(prob[p][:, tiles[t]], prob[p][:, tiles[t]], ACT.Exp, bias=m,
                                                   scale=-1.0)
                    ins.then_inc(s["exp_done"], 1)
                    return
                soft = sum(g["kind"] != "lstm" for g in heads[:i + 1])
                act.wait_ge(s["score_seen"], soft)
                if h["sink"] is not None:
                    sk = sinks(heads)[:, h["sink"]:h["sink"] + 1]
                    nc.scalar.activation(esink[:, p, :], nmx[:, p, :], ACT.Exp, bias=sk)
                for t in range(T):
                    ins = nc.scalar.activation(prob[p][:, tiles[t]], prob[p][:, tiles[t]], ACT.Exp, scale=-1.0,
                                               bias=nmx[:, p, t:t + 1], accum_out=esum[:, p, t:t + 1])
                ins.then_inc(s["exp_done"], 1)

            def copy(i):
                bank, k, _ = fills[i]["tp"]
                act.wait_ge(tp_full[bank], k)
                nc.scalar.copy(probT[:, (i % 2) * GROUP:(i % 2) * GROUP + used], tp[bank][:, 0:used])\
                    .then_inc(s["probT_ready"], 1)

            def pair(i):
                h = heads[i]
                if h["kind"] == "lstm" or h["half"] == 0:
                    return
                bank, k, _ = fills[i]["o"]
                act.wait_ge(acc_full[bank], k)
                nc.scalar.activation(a_hi[:, h["chunk"], :], acc[bank][:, 0:S], ACT.Copy).then_inc(s["pair_hi"], 1)

            for i in range(n + 4):
                if 3 <= i < n + 3:
                    copy(i - 3)
                if i < n:
                    exps(i)
                if beside is not None:
                    beside(i)
                if i >= 4:
                    pair(i - 4)

        FILLS1 = (0, 3, 1, 4, 2)
        TYPES1 = ((0, MOBA, 0), (MOBA, SWA, 2), (MOBA + SWA, MOBA, 1), (2 * MOBA + SWA, SWA_KV, 3))
        RUNS2 = ((0, ZQA, 2 * NA), (2 * NA, ZQS, SW + SW_KV))
        TYPES2 = ((ZQA, NA), (ZKA, NA), (ZQS, SW), (ZKS, SW_KV))

        def by_head(t):
            return t.rearrange("p t (h d) -> p t h d", d=HD)

        def base_const(eng):
            eng.wait_ge(x_in, 16 * T)
            eng.wait_ge(base_in, 16 * len(BASE))

        def copy_heads(hT, kz, f, q_fills, src, tiles):
            if f < q_fills:
                return nc.scalar.copy(hT[:, 2 * f:2 * f + 2, :], src[:, :].rearrange("p (c s) -> p c s", s=S))
            j = 2 * (f - q_fills)
            for i in range(2):
                rows = slice(i * HD, (i + 1) * HD)
                ins = nc.scalar.copy(kz[rows, j:j + tiles, i, :],
                                     src[rows, 0:tiles * S].rearrange("p (c s) -> p c s", s=S))
            return ins

        def act_layer1(act, l):
            b = Book()
            act.dma_start(prow[:, 0:R1], a["prow1"][bass.ds(l, 1)].rearrange("o p n -> (o p) n")
                          .broadcast_to([P, R1])).then_inc(s["rows_in"], 16)
            zero = [0] * RAW

            def split(to):
                act_split(act, b, l, PLAN1, zero, USES1, to)

            act.wait_ge(s["cols_ready"], 1)
            act_next(b, split, act_turn(act, b, C_LN1))
            split(b.unit + RING)
            act_norm(act, b, None)
            for g, (c0, w) in enumerate(groups(IN1)):
                n = len(by_columns("", D, c0, w))
                if g == CONV_AFTER + 1:
                    for f in range(2):
                        bank, k, _ = conv_fill(b)
                        act.wait_ge(tp_full[bank], k)
                        nc.scalar.copy(xT[:, 2 * f:2 * f + 2, :], tp[bank][:, :].rearrange("p (c s) -> p c s", s=S))\
                            .then_inc(s["conv_seen"], 1)
                    gate_fill(b)
                    split(b.unit + 1 + AHEAD)
                    act.wait_ge(s["gate_abs"], 1)
                    tick(act, b, act_chain, nc.scalar.activation(g_e[:, :], g_e[:, :], ACT.Exp))
                    nc.scalar.activation(g_e[:, :], g_e[:, :], ACT.Ln, bias=1.0).then_inc(s["gate_ln"], 1)
                split(b.unit + n + AHEAD)
                full = stream_done(b, (2 * (g % 2), 2 * (g % 2) + 1), n)
                if g == 0:
                    act.wait_ge(s["rstd_ready"], 1)
                for t in range(T):
                    wait(act, full[t])
                    nc.scalar.activation(z1[:, t, c0:c0 + w], acc[2 * (g % 2) + t][:, 0:w], ACT.Identity,
                                         scale=rstd[:, t:t + 1]).then_inc(s["z_act"], 1)
                if g == QK_GROUP:
                    act.wait_ge(s["z_act"], 2 * (g + 1))
                    nc.scalar.activation(sq1[:, :, :], z1[:, :, 0:QK1 * HD], ACT.Square).then_inc(s["sq_ready"], 1)
            act.wait_ge(s["z_act"], 2 * len(groups(IN1)))
            for f in FILLS1:
                bank, k, _ = heads_fill(b)
                act.wait_ge(tp_full[bank], k)
                copy_heads(hT1, kz1, f, 3, tp[bank], 2).then_inc(s["heads_t"], 1)
            gcol_fill(b)

            def beside(i):
                if i == TAPS + 3:
                    zxo = z1[:, :, ZXO:ZXO + LSTM * HD]
                    nc.scalar.activation(zxo, zxo, ACT.Sigmoid).then_inc(s["xo_ready"], 1)
                    act.wait_ge(s["conv_done"], TAPS)
                    nc.scalar.activation(conv_sig[:, :, :], hT1[:, 6:10, :], ACT.Sigmoid)\
                        .then_inc(s["sig_conv"], 1)
                if i == GCOL_AT + 4:
                    act.wait_ge(s["gcol_ready"], 1)
                    nc.scalar.activation(floor[:, :, :], gcol[:, :, 1, :], ACT.Exp).then_inc(s["floor_ready"], 1)

            act_heads(act, b, HEADS1, beside)
            split(b.unit + Y_AT + AHEAD)
            bank, n, _, k = y_fill(b)
            act.wait_ge(tp_full[bank], n)
            nc.scalar.activation(a_hi[:, 3:5, :], tp[bank][:, :].rearrange("p (c s) -> p c s", s=S), ACT.Copy)\
                .then_inc(s["pair_hi"], 1)
            split(b.unit + DC)
            stream_done(b, range(4), DC)
            b.mark("x_new", 4)
            act_next(b, split, act_turn(act, b, C_LN2))
            split(b.unit + RING)
            act_norm(act, b, (s["x_new"], b.marks["x_new"]))
            gs = groups(FF1)
            for g, (c0, w) in enumerate(gs):
                n = len(by_columns("", D, c0, w))
                split(b.unit + n + AHEAD)
                full = stream_done(b, (2 * (g % 2), 2 * (g % 2) + 1), n)
                if g == 0:
                    act.wait_ge(s["rstd_ready"], 2)
                if g >= 2:
                    act.wait_ge(s["act_ready"], g - 1)
                for t in range(T):
                    wait(act, full[t])
                    ins = nc.scalar.activation(act_out[g % 2][:, t, :], acc[2 * (g % 2) + t][:, 0:w], ACT.Relu,
                                               scale=rstd[:, t:t + 1])
                ins.then_inc(s["relu_out"], 1)
                if g:
                    act_hidden(act, b, g - 1, gs[g - 1][1])
            act_hidden(act, b, len(gs) - 1, gs[-1][1])
            split(len(PLAN1))
            layer_end(act, "act", b)

        def dve_layer1(dve, l):
            b = Book()
            nc.vector.tensor_copy(pcol[:, 0:C1], pcol1[:, bass.ds(l, 1), :].rearrange("p o n -> p (o n)"))\
                .then_inc(s["cols_ready"], 1)
            dve.wait_ge(s["cols_ready"], 1)

            def split(to):
                dve_split(dve, b, PLAN1, to)

            dve_next(b, split, None, dve_turn(dve, b, C_LN1))
            split(b.unit + RING)
            dve_norm(dve, b)
            for g, (c0, w) in enumerate(groups(IN1)):
                n = len(by_columns("", D, c0, w))
                if g == CONV_AFTER + 1:
                    conv_fill(b), conv_fill(b)
                    bank, k, _ = gate_fill(b)
                    dve.wait_ge(tp_full[bank], k)
                    nc.vector.tensor_scalar(g_in[:, :], tp[bank][0:LSTM, 0:S], pcol[0:LSTM, C_IB:C_IB + 1], None, ALU.add)
                    nc.vector.tensor_scalar(g_f[:, :], tp[bank][0:LSTM, S:2 * S], pcol[0:LSTM, C_FB:C_FB + 1], None,
                                            ALU.add).then_inc(s["gates_seen"], 1)
                    dve.wait_ge(s["gates_seen"], 1)
                    nc.vector.scalar_tensor_tensor(out=g_e[:, :], in0=g_f[:, :], scalar=-1.0, in1=g_f[:, :], op0=ALU.mult,
                                                   op1=ALU.min).then_inc(s["gate_abs"], 1)
                split(b.unit + min(2, n) + AHEAD)
                if g == 1:
                    dve.wait_ge(const_in, 16 * n_const)
                    dve.wait_ge(s["rows_in"], 16)
                    gain = prow[:, 0:4 * HD].rearrange("p (y d) -> p y d", d=HD)
                    for t in range(T):
                        nc.vector.tensor_tensor(rope_gc[:, t], rope_c[:, t], gain, ALU.mult)
                        for i in range(2):
                            to, frm = slice(i * 32, i * 32 + 32), slice(32 - i * 32, 64 - i * 32)
                            ins = nc.vector.tensor_tensor(rope_gs[:, t, :, to], rope_s[:, t, :, to], gain[:, :, frm],
                                                          ALU.mult)
                    ins.then_inc(s["tables_ready"], 1)
                    nc.vector.tensor_scalar(nsink[:, 0:SWA], prow[:, R_SINK:R_SINK + SWA], -1.0, None, ALU.mult)\
                        .then_inc(s["sink_ready"], 1)
                if g == QK_GROUP + 1:
                    m = T * QK1
                    dve.wait_ge(s["sq_ready"], 1)
                    tick(dve, b, dve_chain, nc.vector.tensor_reduce(ssq[:, 0:m].rearrange("p (t h) -> p t h", t=T),
                                                                    by_head(sq1[:, :, :]), X, ALU.add))
                    nc.vector.tensor_scalar(msq[:, 0:m], ssq[:, 0:m], 1.0 / HD, EPS, ALU.mult, ALU.add)\
                        .then_inc(s["ms_ready"], 1)
                if g == CONV_AFTER:
                    dve.wait_ge(s["rope_a_ready"], 1)
                    dve.wait_ge(s["rope_b_ready"], 1)
                    nc.vector.tensor_tensor(qk[:, :, :], qk[:, :, :], qk_b[:, :, :], ALU.add)\
                        .then_inc(s["rope_sum"], 1)
                split(b.unit + n + AHEAD)
                if g == QK_GROUP + 1:
                    dve.wait_ge(s["z_act"], 2 * (QK_GROUP + 1))
                    dve.wait_ge(s["tables_ready"], 1)
                    for h0, nh, y in TYPES1:
                        for t in range(T):
                            ins = nc.vector.tensor_tensor(by_head(qk[:, :, :])[:, t, h0:h0 + nh, :],
                                                          by_head(z1[:, :, 0:QK1 * HD])[:, t, h0:h0 + nh, :],
                                                          rope_gc[:, t, y:y + 1, :].broadcast_to([P, nh, HD]), ALU.mult)
                    ins.then_inc(s["rope_a_ready"], 1)
                if g == CONV_AFTER:
                    dve.wait_ge(s["rope_sum"], 1)
                    dve.wait_ge(s["rsh_ready"], 1)
                    qh = qk[:, :, :].rearrange("p t (h d) -> p (t h) d", d=HD)
                    nc.vector.tensor_tensor(qh, qh, rstd_h[:, 0:T * QK1].unsqueeze(2).broadcast_to([P, T * QK1, HD]),
                                            ALU.mult).then_inc(s["qk_ready"], 1)
                stream_done(b, (2 * (g % 2), 2 * (g % 2) + 1), n)
            for f in range(5):
                heads_fill(b)
            bank, gcol_full, _ = gcol_fill(b)

            def lstm_inputs(i):
                if i == 0:
                    dve.wait_ge(s["conv_seen"], 2)
                if i < TAPS:
                    for c in range(4):
                        wcol = pcol[:, C_CONV + c * TAPS + TAPS - 1 - i:C_CONV + c * TAPS + TAPS - i]
                        if i == 0:
                            ins = nc.vector.tensor_scalar(hT1[:, 6 + c, :], xT[:, c, :], wcol,
                                                          pcol[:, C_CONVB + c:C_CONVB + c + 1], ALU.mult, ALU.add)
                        else:
                            if c == 0:
                                dve.wait_ge(s["conv_done"], i)
                            ins = nc.vector.scalar_tensor_tensor(out=hT1[:, 6 + c, i:S], in0=xT[:, c, 0:S - i],
                                                                 scalar=wcol, in1=hT1[:, 6 + c, i:S], op0=ALU.mult,
                                                                 op1=ALU.add)
                    ins.then_inc(s["conv_done"], 1)
                if i == 4:
                    dve.wait_ge(s["gate_ln"], 1)
                    tick(dve, b, dve_chain, nc.vector.scalar_tensor_tensor(
                        out=g_f[:, :], in0=g_f[:, :], scalar=0.0, in1=g_e[:, :], op0=ALU.min, op1=ALU.subtract))
                    tick(dve, b, dve_chain, nc.vector.tensor_tensor_scan(g_cum[:, :], ones[:, :], g_f[:, :], 0.0,
                                                                         ALU.mult, ALU.add))
                if i == 5:
                    tick(dve, b, dve_chain, nc.vector.tensor_tensor(g_u[:, :], g_in[:, :], g_cum[:, :],
                                                                    ALU.subtract))
                    tick(dve, b, dve_chain, nc.vector.tensor_tensor_scan(g_m[:, :], g_u[:, :], g_u[:, :], 0.0,
                                                                         ALU.max, ALU.max))
                if i == 6:
                    nc.vector.tensor_scalar(g_row[:, 0, :], g_m[:, :], -1.0, None, ALU.mult)
                    nc.vector.scalar_tensor_tensor(out=g_row[:, 1, :], in0=g_cum[:, :], scalar=-1.0, in1=g_m[:, :],
                                                   op0=ALU.mult, op1=ALU.subtract).then_inc(s["gate_rows"], 1)
                if i == GCOL_AT + 3:
                    dve.wait_ge(acc_full[bank], gcol_full)
                    nc.vector.tensor_copy(gcol[:, :, :, :].rearrange("p t i h -> p (t i h)"),
                                          acc[bank][:, 0:4 * LSTM]).then_inc(s["gcol_ready"], 1)

            dve_heads(dve, b, HEADS1, lstm_inputs)
            dve.wait_ge(s["prob_ready"], len(HEADS1))
            dve.wait_ge(s["floor_ready"], 1)
            tick(dve, b, dve_chain, nc.vector.scalar_tensor_tensor(out=dabs[:, :, :], in0=den[:, :, :], scalar=-1.0,
                                                                   in1=den[:, :, :], op0=ALU.mult, op1=ALU.max))
            tick(dve, b, dve_chain, nc.vector.tensor_tensor(dabs[:, :, :], dabs[:, :, :], floor[:, :, :], ALU.max))
            tick(dve, b, dve_chain, nc.vector.reciprocal(drec[:, :, :], dabs[:, :, :]))
            dve.wait_ge(s["units_used"], b.unit)
            dve.wait_ge(acc_full[2], b.marks["acc_full2"])
            m = T * LSTM
            nc.vector.tensor_tensor(lstm_h[:, :, :].rearrange("p t (h d) -> p (t h) d", d=HD),
                                    acc[2][:, :].rearrange("p (m d) -> p m d", d=HD),
                                    drec[:, :, :].rearrange("p t h -> p (t h)").unsqueeze(2).broadcast_to([P, m, HD]),
                                    ALU.mult).then_inc(s["lstm_seen"], 1)
            dve.wait_ge(s["lstm_seen"], 1)
            dve.wait_ge(s["xo_ready"], 1)
            tick(dve, b, dve_chain, nc.vector.tensor_tensor(lstm_h[:, :, :], lstm_h[:, :, :],
                                                            z1[:, :, ZXO:ZXO + LSTM * HD], ALU.mult))
            tick(dve, b, dve_chain, nc.vector.tensor_tensor(lstm_q[:, :, :], lstm_h[:, :, :], lstm_h[:, :, :], ALU.mult))
            tick(dve, b, dve_chain, nc.vector.tensor_reduce(ssq[:, 0:m].rearrange("p (t h) -> p t h", t=T),
                                                            by_head(lstm_q[:, :, :]), X, ALU.add))
            nc.vector.tensor_scalar(msq[:, 0:m], ssq[:, 0:m], 1.0 / HD, EPS, ALU.mult, ALU.add)\
                .then_inc(s["ms_ready"], 1)
            split(b.unit + RING)
            dve.wait_ge(s["rsh_ready"], 2)
            hh = lstm_h[:, :, :].rearrange("p t (h d) -> p (t h) d", d=HD)
            tick(dve, b, dve_chain, nc.vector.tensor_tensor(hh, hh, rstd_h[:, 0:m].unsqueeze(2)
                                                            .broadcast_to([P, m, HD]), ALU.mult))
            g = prow[:, R_MN:R_MN + LSTM * HD].unsqueeze(1).broadcast_to([P, T, LSTM * HD])
            nc.vector.tensor_tensor(lstm_h[:, :, :], lstm_h[:, :, :], g, ALU.mult).then_inc(s["y_ready"], 1)
            split(b.unit + Y_AT + AHEAD)
            bank, n, _, k = y_fill(b)
            dve.wait_ge(s["pair_hi"], k)
            nc.vector.tensor_tensor(a_lo[:, 3:5, :], tp[bank][:, :].rearrange("p (c s) -> p c s", s=S),
                                    a_hi[:, 3:5, :].bitcast(F32), ALU.subtract).then_inc(s["pair_lo"], 1)
            split(b.unit + DC)
            dve_next(b, split, dve_add_x(dve, b, 1.0, DC), dve_turn(dve, b, C_LN2))
            split(b.unit + RING)
            dve_norm(dve, b)
            gs = groups(FF1)
            for g, (c0, w) in enumerate(gs):
                n = len(by_columns("", D, c0, w))
                split(b.unit + n + AHEAD)
                stream_done(b, (2 * (g % 2), 2 * (g % 2) + 1), n)
                dve.wait_ge(s["relu_out"], g + 1)
                r = act_out[g % 2][:, :, :]
                nc.vector.tensor_tensor(r, r, r, ALU.mult).then_inc(s["act_ready"], 1)
                b.mark("act_ready")
                if g:
                    dve_hidden(dve, b, g - 1, gs[g - 1][1])
            dve_hidden(dve, b, len(gs) - 1, gs[-1][1])
            split(len(PLAN1))
            dve_add_x(dve, b, 1.0, FF1 // P)(4)
            dve.wait_ge(s["x_new"], b.marks["x_new"])
            layer_end(dve, "dve", b)

        def pool_layer1(pool):
            b = Book()
            pool_norm(pool, b)
            pool.wait_ge(s["tables_ready"], 1)
            pool.wait_ge(s["z_act"], 2 * (QK_GROUP + 1))
            for h0, n, y in TYPES1:
                zz = by_head(z1[:, :, 0:QK1 * HD])[:, :, h0:h0 + n, :]
                for t in range(T):
                    for i in range(2):
                        to, frm = slice(i * 32, i * 32 + 32), slice(32 - i * 32, 64 - i * 32)
                        ins = nc.gpsimd.tensor_tensor(by_head(qk_b[:, :, :])[:, t, h0:h0 + n, to], zz[:, t, :, frm],
                                                      rope_gs[:, t, y:y + 1, to].broadcast_to([P, n, 32]), ALU.mult)
            ins.then_inc(s["rope_b_ready"], 1)
            pool.wait_ge(s["ms_ready"], 1)
            m = T * QK1
            nc.gpsimd.tensor_tensor(rstd_h[:, 0:m], msq[:, 0:m], half[:, 0:m], ALU.pow).then_inc(s["rsh_ready"], 1)
            pool.wait_ge(s["rope_sum"], 1)
            pool.wait_ge(s["rsh_ready"], 1)
            zero_halves(kz1)
            pool.wait_ge(s["kz_ready"], 1)
            pool.wait_ge(s["sig_conv"], 1)
            nc.gpsimd.tensor_tensor(hT1[:, 6:8, :], hT1[:, 6:8, :], conv_sig[:, 0:2, :], ALU.mult)\
                .then_inc(s["silu_conv"], 1)
            pool.wait_ge(s["silu_conv"], 1)
            for j in range(2):
                rows = slice(j * HD, (j + 1) * HD)
                nc.gpsimd.tensor_tensor(kz1[rows, 4:6, j, :], hT1[rows, 8:10, :], conv_sig[rows, 2:4, :], ALU.mult)\
                    .then_inc(s["silu_conv"], 1)
            pool.wait_ge(s["silu_conv"], 3)
            pool.wait_ge(s["ms_ready"], 2)
            m = T * LSTM
            nc.gpsimd.tensor_tensor(rstd_h[:, 0:m], msq[:, 0:m], half[:, 0:m], ALU.pow).then_inc(s["rsh_ready"], 1)
            pool_norm(pool, b)
            pool_end(pool)

        def pool_end(pool):
            pool.wait_ge(layer_done, 3)
            pool.sem_clear(range(min(nums), max(nums) + 1))
            for e in go.values():
                pool.sem_inc(e, 1)

        FG2 = groups(FF2)

        def pe_ffn2(pe, b, turn, turn_next):
            hid0 = b.marks.get("hid", 0)
            for g, (c0, w) in enumerate(FG2):
                n = len(by_columns("", D, c0, w))
                k = b.mark("silu")
                pe_stream(pe, b, PLAN2, n, a_hi, a_lo, [0, 1], [(s["silu_done"], k)] * 2,
                          turned(b, turn) if g == 0 else None)
                if g:
                    pe_hidden(pe, b, g - 1, FG2[g - 1][1])
                pe_stream(pe, b, PLAN2, n, a_hi, a_lo, [2, 3], [(s["act_ready"], k)] * 2)
            pe_hidden(pe, b, len(FG2) - 1, FG2[-1][1])
            b_x = released_x(b)
            if turn_next:
                turn = pe_turn(pe, b, x_chunk, x_need(b, 4))
            pe_stream(pe, b, PLAN2, FF2 // P, h_hi, h_lo, range(4), b_x,
                      lambda n: (s["hid_lo"], hid0 + n // 2 + 1) if n % 2 == 0 else None,
                      late=(lambda: turn(2)) if turn_next else None)
            b.mark("x_new", 4)
            return turn

        def act_ffn2(act, b, l, base, need):
            gain = b.mark("ffn") - 1

            def split(to):
                act_split(act, b, l, PLAN2, base, USES2, to)

            act_next(b, split, act_turn(act, b, 2 * DC * gain))
            split(b.unit + RING)
            act_norm(act, b, need)
            rn = b.marks["norm"]
            for g, (c0, w) in enumerate(FG2):
                n = len(by_columns("", D, c0, w))
                act_split(act, b, l, PLAN2, base, USES2, b.unit + n + AHEAD)
                full = stream_done(b, (0, 1), n)
                if g == 0:
                    act.wait_ge(s["rstd_ready"], rn)
                k = b.mark("silu")
                if k > 1:
                    act.wait_ge(s["act_ready"], k - 1)
                for t in range(T):
                    wait(act, full[t])
                    ins = nc.scalar.activation(silu_out[:, t, 0:w], acc[t][:, 0:w], ACT.Silu, scale=rstd[:, t:t + 1])
                ins.then_inc(s["silu_done"], 1)
                if g:
                    act_hidden(act, b, g - 1, FG2[g - 1][1])
                act_split(act, b, l, PLAN2, base, USES2, b.unit + n + AHEAD)
                stream_done(b, (2, 3), n)
            act_hidden(act, b, len(FG2) - 1, FG2[-1][1])
            act_split(act, b, l, PLAN2, base, USES2, b.unit + FF2 // P)
            stream_done(b, range(4), FF2 // P)
            b.mark("x_new", 4)

        def dve_ffn2(dve, b, add):
            gain = b.mark("ffn") - 1

            def split(to):
                dve_split(dve, b, PLAN2, to)

            dve_next(b, split, add, dve_turn(dve, b, 2 * DC * gain))
            split(b.unit + RING)
            dve_norm(dve, b)
            rn = b.marks["norm"]
            for g, (c0, w) in enumerate(FG2):
                n = len(by_columns("", D, c0, w))
                dve_split(dve, b, PLAN2, b.unit + n + AHEAD)
                stream_done(b, (0, 1), n)
                if g:
                    dve_hidden(dve, b, g - 1, FG2[g - 1][1])
                dve_split(dve, b, PLAN2, b.unit + n + AHEAD)
                full = stream_done(b, (2, 3), n)
                dve.wait_ge(s["silu_done"], b.mark("silu"))
                if g == 0:
                    dve.wait_ge(s["rstd_ready"], rn)
                for t in range(T):
                    wait(dve, full[t])
                    ins = nc.vector.scalar_tensor_tensor(out=act_out[g % 2][:, t, 0:w], in0=acc[2 + t][:, 0:w],
                                                         scalar=rstd[:, t:t + 1], in1=silu_out[:, t, 0:w],
                                                         op0=ALU.mult, op1=ALU.mult)
                ins.then_inc(s["act_ready"], 1)
            dve_hidden(dve, b, len(FG2) - 1, FG2[-1][1])
            dve_split(dve, b, PLAN2, b.unit + FF2 // P)
            return dve_add_x(dve, b, 0.5, FF2 // P)

        NG2 = len(IN2_GROUPS)
        PLAIN2 = len(groups(ZG))
        Z_DVE2 = PLAIN2 + 2 * (NG2 - PLAIN2)

        def z2_released(g):
            if g < PLAIN2:
                return [(s["z_act"], g + 1), (s["z_dve"], g + 1)]
            k = PLAIN2 + 2 * (g - PLAIN2)
            return [(s["z_dve"], k + 1), (s["z_dve"], k + 2)]

        TILES2 = [c + i * P for c in (ZQA, ZQS, ZKA) for i in range(4)] + [ZKS]
        HEADS_AFTER = PLAIN2 + 2

        def pe_layer2(pe):
            b = Book()
            turn = pe_turn(pe, b, x_chunk, lambda f: None)
            turn(2)
            turn = pe_ffn2(pe, b, turn, True)
            for g, (c0, w) in enumerate(IN2_GROUPS):
                pe_stream(pe, b, PLAN2, len(by_columns("", D, c0, w)), a_hi, a_lo, [2 * (g % 2), 2 * (g % 2) + 1],
                          z2_released(g), turned(b, turn) if g == 0 else None)
                if g != HEADS_AFTER:
                    continue
                pe.wait_ge(s["normed"], 1)
                for f in range(7):
                    bank, n, before = heads_fill(b)
                    wait(pe, before)
                    for i, c in enumerate(TILES2[2 * f:2 * f + 2]):
                        for t in range(T):
                            mm = nc.tensor.transpose(tp[bank][:, i * S + t * P:i * S + (t + 1) * P],
                                                     z2[:, t, c:c + P], ident[:, :])
                    mm.then_inc(tp_full[bank], 1)
            na_step = pe_steps(pe, b, PLAN2, 2, a_hi, a_lo, [0, 1], [(s["na_out"], 1)] * 2,
                               lambda n: (s["pair_lo"], NAW // P))
            pe_heads(pe, b, HEADS2, None, lambda i: na_step() if i in (len(HEADS2) - 2, len(HEADS2) - 1) else None)
            turn = pe_turn(pe, b, lambda t, c: work[:, t * D + c * P:t * D + (c + 1) * P],
                           lambda f: (s["merged"], f // 2 + 1))
            for n in range(2):
                if n == 1:
                    pe_stream(pe, b, PLAN2, 2, a_hi, a_lo, [0, 1], [(s["na_out"], n + 1)] * 2)
                    turn(2)
                pe_stream(pe, b, PLAN2, 2, a_hi, a_lo, [2, 3], [(s["sw_out"], n + 1)] * 2,
                          lambda i: (s["pair_lo"], (NAW + SWQW) // P), NAW // P)
            b_x = released_x(b)
            next_turn = pe_turn(pe, b, x_chunk, x_need(b, 4))
            pe_stream(pe, b, PLAN2, DC, a_hi, a_lo, range(4), b_x, turned(b, turn, 1, b.turns - 4),
                      late=lambda: next_turn(2))
            b.mark("x_new", 4)
            pe_ffn2(pe, b, next_turn, False)
            pe.wait_ge(s["units_used"], b.unit)
            layer_end(pe, "pe", b)

        def act_layer2(act, l):
            b = Book()
            base = [DEPTH * u for u in USES1]
            act.dma_start(prow[:, 0:R2], a["prow2"][bass.ds(l, 1)].rearrange("o p n -> (o p) n")
                          .broadcast_to([P, R2])).then_inc(s["rows_in"], 16)

            def split(to):
                act_split(act, b, l, PLAN2, base, USES2, to)

            act.wait_ge(s["cols_ready"], 1)
            act_ffn2(act, b, l, base, None)
            act_next(b, split, act_turn(act, b, DC))
            act.wait_ge(s["x_new"], b.marks["x_new"])
            act.dma_start(na_bias[:, :, :, :], na_skew[bass.ds(l, 1)].rearrange("o p t h k -> (o p) t h k"))\
                .then_inc(s["bias_in"], 16)
            split(b.unit + RING)
            act_norm(act, b, (s["x_new"], b.marks["x_new"]))
            rn = b.marks["norm"]
            for g, (c0, w) in enumerate(IN2_GROUPS):
                n = len(by_columns("", D, c0, w))
                if g == HEADS_AFTER + 1:
                    for f in range(7):
                        bank, k, _ = heads_fill(b)
                        m = len(TILES2[2 * f:2 * f + 2])
                        act.wait_ge(tp_full[bank], k)
                        copy_heads(hT2, kz2, f, 4, tp[bank], m).then_inc(s["heads_t"], 1)
                act_split(act, b, l, PLAN2, base, USES2, b.unit + n + AHEAD)
                full = stream_done(b, (2 * (g % 2), 2 * (g % 2) + 1), n)
                if g == 0:
                    act.wait_ge(s["rstd_ready"], rn)
                if g < PLAIN2:
                    wait(act, full[0])
                    nc.scalar.activation(z2[:, 0, c0:c0 + w], acc[2 * (g % 2)][:, 0:w], ACT.Identity,
                                         scale=rstd[:, 0:1]).then_inc(s["z_act"], 1)
                if g == PLAIN2 - 1:
                    act.wait_ge(s["z_act"], PLAIN2)
                    act.wait_ge(s["z_dve"], PLAIN2)
                    for h0, c1, m in RUNS2:
                        ins = nc.scalar.activation(sq2[:, :, h0 * HD:(h0 + m) * HD], z2[:, :, c1:c1 + m * HD],
                                                   ACT.Square)
                    ins.then_inc(s["sq_ready"], 1)
            act.wait_ge(s["z_dve"], Z_DVE2)
            act_heads(act, b, HEADS2)
            split(b.unit + RING + 1)
            zg = z2[:, :, ZG:ZG + 2 * D].rearrange("p t (i n c) -> p t i n c", i=2, n=2)
            for n in range(2):
                nc.scalar.activation(zg[:, :, :, n, :], zg[:, :, :, n, :], ACT.Sigmoid).then_inc(s["g_ready"], 1)
                split(b.unit + RING + 2)
            split(b.unit + 8 + 1)
            for n in range(2):
                stream_done(b, (0, 1), 2)
                stream_done(b, (2, 3), 2)
            act_next(b, split, act_turn(act, b, None), 1)
            split(b.unit + DC)
            stream_done(b, range(4), DC)
            b.mark("x_new", 4)
            act_ffn2(act, b, l, base, (s["x_new"], b.marks["x_new"]))
            layer_end(act, "act", b)

        def dve_layer2(dve, l):
            b = Book()
            nc.vector.tensor_copy(pcol[:, 0:C2], pcol2[:, bass.ds(l, 1), :].rearrange("p o n -> p (o n)"))\
                .then_inc(s["cols_ready"], 1)
            dve.wait_ge(s["cols_ready"], 1)

            def split(to):
                dve_split(dve, b, PLAN2, to)

            add = dve_ffn2(dve, b, None)
            dve_next(b, split, add, dve_turn(dve, b, DC))
            split(b.unit + RING)
            dve_norm(dve, b)
            rn = b.marks["norm"]
            nh = 2 * NA + SW + SW_KV
            for g, (c0, w) in enumerate(IN2_GROUPS):
                n = len(by_columns("", D, c0, w))
                split(b.unit + min(2, n) + AHEAD)
                if g == PLAIN2:
                    dve.wait_ge(s["rows_in"], 16)
                    for y in range(4):
                        ins = nc.vector.tensor_scalar(gain2[:, y, :], prow[:, R2_GAIN + y * HD:R2_GAIN + (y + 1) * HD],
                                                      -HD ** -0.5 if y % 2 == 0 else 1.0, None, ALU.mult)
                    nc.vector.tensor_scalar(nsink[:, 0:SW], prow[:, R2_SINK:R2_SINK + SW], -1.0, None, ALU.mult)\
                        .then_inc(s["sink_ready"], 1)
                    dve.wait_ge(s["sq_ready"], 1)
                    tick(dve, b, dve_chain, nc.vector.tensor_reduce(ssq[:, 0:T * nh].rearrange("p (t h) -> p t h", t=T),
                                                                    by_head(sq2[:, :, :]), X, ALU.add))
                    nc.vector.tensor_scalar(msq[:, 0:T * nh], ssq[:, 0:T * nh], 1.0 / HD, EPS, ALU.mult, ALU.add)\
                        .then_inc(s["ms_ready"], 1)
                if g == PLAIN2 + 1:
                    dve.wait_ge(s["rsh_ready"], 1)
                    for h0, c1, m in RUNS2:
                        zz = by_head(z2[:, :, c1:c1 + m * HD])
                        r = rstd_h[:, 0:T * nh].rearrange("p (t h) -> p t h", t=T)[:, :, h0:h0 + m]
                        ins = nc.vector.tensor_tensor(zz, zz, r.unsqueeze(3).broadcast_to([P, T, m, HD]), ALU.mult)
                    tick(dve, b, dve_chain, ins)
                if g == PLAIN2 + 2:
                    for y, (c1, m) in enumerate(TYPES2):
                        for t in range(T):
                            zz = by_head(z2[:, :, c1:c1 + m * HD])[:, t]
                            ins = nc.vector.tensor_tensor(zz, zz, gain2[:, y:y + 1, :].broadcast_to([P, m, HD]),
                                                          ALU.mult)
                    ins.then_inc(s["normed"], 1)
                split(b.unit + n + AHEAD)
                full = stream_done(b, (2 * (g % 2), 2 * (g % 2) + 1), n)
                if g == 0:
                    dve.wait_ge(s["rstd_ready"], rn)
                for t in range(T):
                    k = acc[2 * (g % 2) + t][:, 0:w]
                    if g < PLAIN2 and t == 1:
                        wait(dve, full[t])
                        nc.vector.tensor_scalar(z2[:, t, c0:c0 + w], k, rstd[:, t:t + 1], None, ALU.mult)\
                            .then_inc(s["z_dve"], 1)
                    elif g >= PLAIN2:
                        wait(dve, full[t])
                        bg = prow[:, R2_BG + c0 - ZG:R2_BG + c0 - ZG + w]
                        nc.vector.scalar_tensor_tensor(out=z2[:, t, c0:c0 + w], in0=k, scalar=rstd[:, t:t + 1], in1=bg,
                                                       op0=ALU.mult, op1=ALU.add).then_inc(s["z_dve"], 1)
            for f in range(7):
                heads_fill(b)
            dve.wait_ge(t5_in, 16)
            dve.wait_ge(s["bias_ready"], 1)
            dve_heads(dve, b, HEADS2)
            turn = dve_turn(dve, b, None)
            for n in range(2):
                for i, done in ((0, "na_out"), (2, "sw_out")):
                    split(b.unit + 2 + (AHEAD if n == 0 else 1))
                    if i == 0:
                        dve.wait_ge(s["g_ready"], n + 1)
                    elif n == 1:
                        turn(2)
                    full = stream_done(b, (i, i + 1), 2)
                    for t in range(T):
                        wait(dve, full[t])
                        c = ZG + (i // 2) * D + n * GROUP
                        to = work[:, t * D + n * GROUP:t * D + (n + 1) * GROUP] if i == 0 else act_out[0][:, t, :]
                        ins = nc.vector.tensor_tensor(to, acc[i + t][:, :], z2[:, t, c:c + GROUP], ALU.mult)
                    ins.then_inc(s[done], 1)
                dve.wait_ge(s["sw_out"], n + 1)
                both = work[:, :].rearrange("p (t d) -> p t d", t=T)[:, :, n * GROUP:(n + 1) * GROUP]
                nc.vector.tensor_tensor(both, both, act_out[0][:, :, :], ALU.add).then_inc(s["merged"], 1)
                dve.wait_ge(s["merged"], n + 1)
            split(b.unit + 3)
            turn(1)
            split(b.unit + 4)
            turn(1)
            split(b.unit + DC)
            dve_ffn2(dve, b, dve_add_x(dve, b, 1.0, DC))(4)
            dve.wait_ge(s["x_new"], b.marks["x_new"])
            layer_end(dve, "dve", b)

        def pool_layer2(pool):
            b = Book()
            pool_norm(pool, b)
            pool_norm(pool, b)
            pool.wait_ge(s["bias_in"], 16)
            nb = na_bias[:, :, :, :].rearrange("p t h k -> p (t h) k")
            nc.gpsimd.tensor_tensor(nb, mask_n[:, :].unsqueeze(1).broadcast_to([P, T * NA, S]), nb, ALU.subtract)\
                .then_inc(s["bias_ready"], 1)
            pool.wait_ge(s["ms_ready"], 1)
            nc.gpsimd.tensor_tensor(rstd_h[:, 0:T * 26], msq[:, 0:T * 26], half[:, 0:T * 26], ALU.pow)\
                .then_inc(s["rsh_ready"], 1)
            pool.wait_ge(s["rsh_ready"], 1)
            zero_halves(kz2)
            pool_norm(pool, b)
            pool_end(pool)

        @blk.tensor
        def _(pe):
            base_const(pe)
            with pe.Fori(0, DEPTH):
                pe_layer1(pe)
            nc.tensor.matmul(acc[0][0:SW, :], t5_tab[:, :], onehot[:, :], start=True, stop=True).then_inc(t5_read, 1)
            pe.wait_ge(t5_row, 1)
            with pe.Fori(0, DEPTH):
                pe_layer2(pe)

        @blk.scalar
        def _(act):
            base_const(act)
            with act.Fori(0, DEPTH) as l:
                act_layer1(act, l)
            act.wait_ge(skewed, 16 * DEPTH * GRID_H * GRID_H)
            with act.Fori(0, DEPTH) as l:
                act_layer2(act, l)

        @blk.vector
        def _(dve):
            base_const(dve)
            with dve.Fori(0, DEPTH) as l:
                dve_layer1(dve, l)
            dve.wait_ge(t5_read, 1)
            nc.vector.tensor_copy(t5_rel[:, :], acc[0][0:SW, :]).then_inc(t5_row, 1)
            with dve.Fori(0, DEPTH) as l:
                dve_layer2(dve, l)
            dve.sem_inc(x_final, 1)

        @blk.gpsimd
        def _(pool):
            base_const(pool)
            with pool.Fori(0, DEPTH):
                pool_layer1(pool)
            pool.wait_ge(t5_row, 1)
            pool.dma_start(t5_dram, t5_rel[:, :]).then_inc(t5_out, 16)
            pool.wait_ge(t5_out, 16)
            for t in range(T):
                src = bass.AP(t5_dram.tensor, S - 1 - t * P, [[REL, SW], [-1, P], [1, S]])
                pool.dma_start(t5_skew[:, t, :, :].rearrange("p h k -> h p k"), src).then_inc(t5_turned, 16)
            pool.wait_ge(t5_turned, 16 * T)
            pool.dma_start(t5_bias[:, :, :, :], t5_skew).then_inc(t5_in, 16)
            with pool.Fori(0, DEPTH):
                pool_layer2(pool)


def constants():
    f = np.float32
    c = {"ident": np.eye(P, dtype=f), "neg_half": np.full((P, 64), -0.5, f), "ones": np.ones((LSTM, S), f)}
    inv = f(10000.0) ** (-np.arange(0, HD, 2, dtype=f) / f(HD))
    ang = np.arange(S, dtype=f)[:, None] * inv[None, :]
    cos, sin = np.cos(ang), np.sin(ang)
    scale = np.array([-HD ** -0.5, 1, -HD ** -0.5, 1], f)

    def by_tile(v):
        return np.ascontiguousarray(v.reshape(T, P, *v.shape[1:]).swapaxes(0, 1))

    c["rope_c"] = by_tile(np.concatenate([cos, cos], -1)[:, None] * scale[:, None])
    c["rope_s"] = by_tile(np.concatenate([-sin, sin], -1)[:, None] * scale[:, None])
    q, k = np.arange(P)[:, None], np.arange(P)[None, :]
    own = np.where(k <= q, 0, MASK).astype(f)
    c["mask_m"] = np.concatenate([own, np.zeros((P, P), f), own], 1)
    c["mask_s"] = np.concatenate([own, np.where(q + P - k < WINDOW1, 0, MASK).astype(f), own], 1)
    c["pick"] = np.repeat(-np.eye(LSTM, dtype=f)[:, :, None], P, 2)
    qc, kc = np.arange(P)[:, None] % GRID_W, np.arange(S)[None, :] % GRID_W
    first = np.clip(qc - NA_COLS // 2, 0, GRID_W - NA_COLS)
    c["mask_n"] = np.where((kc >= first) & (kc < first + NA_COLS), 0, MASK).astype(f)
    rel = np.arange(REL) - (S - 1)
    nb = BUCKETS // 2
    exact = nb // 2
    n = np.abs(rel)
    large = exact + (np.log(np.maximum(n, 1) / exact) / np.log(MAX_DIST / exact) * (nb - exact)).astype(np.int32)
    bucket = (rel > 0) * nb + np.where(n < exact, n, np.minimum(large, nb - 1))
    outside = np.where(n <= WINDOW2, 0, MASK)
    c["onehot"] = np.concatenate([-(np.arange(BUCKETS)[:, None] == bucket[None, :]).astype(f),
                                  outside[None].astype(f)])
    return c


def reordered(w, axis, first, order):
    idx = np.arange(w.shape[axis])
    idx[first:first + len(order) * HD] = (first + np.array(order)[:, None] * HD + np.arange(HD)).ravel()
    return np.take(w, idx, axis)


def slabs(plan, weights):
    outs = np.zeros((DEPTH, len(plan) // 2, P, 2, HALF), np.float32)
    for u, (name, chunks, c0, w) in enumerate(plan):
        k0 = chunks[0]
        part = weights[name][:, k0 * P:(k0 + len(chunks)) * P, c0:c0 + w]
        part = part.reshape(DEPTH, len(chunks), P, w).transpose(0, 2, 1, 3)
        outs[:, u // 2, :, u % 2, :len(chunks) * w] = part.reshape(DEPTH, P, len(chunks) * w)
    return outs.reshape(-1, P, SLAB)


def columns(*parts):
    return np.concatenate([v.reshape(DEPTH, -1, P).transpose(2, 0, 1) for v in parts], 2)


def kernel(**inputs):
    from concourse import bacc
    from concourse.bass_utils import run_bass_kernel_spmd

    i = {k: np.ascontiguousarray(v) for k, v in inputs.items()}
    first = {n: sum(w for _, w in PARTS1[:k]) for k, (n, _) in enumerate(PARTS1)}
    i["w_in"] = reordered(i["w_in"], 2, first["sq"], SWA_ORDER)
    i["w_in"] = np.concatenate([i["w_in"][:, :, first[n]:first[n] + WIDTH1[n]] for n in ORDER1], 2)
    i["w_out"] = reordered(i["w_out"], 1, MOBA * HD + LSTM * HD, SWA_ORDER)
    i["w_in_2"] = reordered(i["w_in_2"], 2, ZQS, SW_ORDER)
    i["w_branch_sw_2"] = reordered(i["w_branch_sw_2"], 1, 0, SW_ORDER)
    f = np.float32
    gates = np.zeros((P, DEPTH, 2), f)
    gates[:LSTM, :, 0], gates[:LSTM, :, 1] = i["igate_b"].T, i["fgate_b"].T
    taps = i["conv_w"].reshape(DEPTH, TAPS, 4, P).transpose(3, 0, 2, 1).reshape(P, DEPTH, 4 * TAPS)
    arrays = {
        "x": i["x"],
        "slabs1": slabs(PLAN1, i), "slabs2": slabs(PLAN2, i),
        "pcol1": np.concatenate([columns(i["ln1"], i["ln2"]), taps, columns(i["conv_b"]), gates], 2),
        "pcol2": columns(i["ffn1_norm_2"], i["mix_norm_2"], i["ffn2_norm_2"]),
        "prow1": np.concatenate([i[k].reshape(DEPTH, 1, -1) for k in (
            "moba_q_norm", "moba_k_norm", "swa_q_norm", "swa_k_norm", "mlstm_norm", "swa_sinks")], 2),
        "prow2": np.concatenate([i[k].reshape(DEPTH, 1, -1) for k in (
            "b_gate_2", "na_q_norm_2", "na_k_norm_2", "sw_q_norm_2", "sw_k_norm_2", "sw_sink_2")], 2),
        "rpb": i["na_rpb_2"], "t5_rel_table_2": i["t5_rel_table_2"], **constants(),
    }
    nc = bacc.Bacc("TRN2", target_bir_lowering=False, num_devices=1)
    aps = {k: nc.dram_tensor(f"in_{k}", v.shape, mybir.dt.from_np(v.dtype), kind="ExternalInput").ap()
           for k, v in arrays.items()}
    out = nc.dram_tensor("out_x", (1, S, D), F32, kind="ExternalOutput").ap()
    build(nc, aps, out)
    r = run_bass_kernel_spmd(nc, [{f"in_{k}": np.ascontiguousarray(v) for k, v in arrays.items()}], core_ids=[0])
    return r.results[0]["out_x"]
```
